# Optimizing a Trainium2 kernel written in Bass

```python
import math
import jax, jax.numpy as jnp
from jax import lax
import numpy as np

D_MODEL = 1024
BATCH = 1
SEQ = 512
DEPTH = 1
DEC_BATCH = 8
DEC_SEQ = 8
PAST_LEN = 4096
PAGE_SIZE = 128

GLA_HEADS = 4
GLA_DK = (D_MODEL // 2) // GLA_HEADS
GLA_DV = D_MODEL // GLA_HEADS
GLA_GATE_RANK = 16
GLA_TAU = 16.0
HGRN_EXPAND = 128
HGRN_HEADS = D_MODEL // HGRN_EXPAND
HGRN_DV = D_MODEL // HGRN_HEADS
LB_FLOOR = 1e-20
D_FF = ((8 * D_MODEL // 3 + 255) // 256) * 256
CHUNK = 64
EPS = 1e-6

SPLIT_SIZES = (
    GLA_HEADS * GLA_DK,
    GLA_HEADS * GLA_DK,
    GLA_HEADS * GLA_DV,
    GLA_HEADS * GLA_DV,
    GLA_GATE_RANK,
    HGRN_HEADS * HGRN_EXPAND,
    HGRN_HEADS * HGRN_EXPAND,
    HGRN_HEADS * HGRN_DV,
    HGRN_HEADS * HGRN_DV,
    D_MODEL,
    D_MODEL,
)
D_IN = sum(SPLIT_SIZES)

kernel_name = "gla_hgrn2_parallel_decoder_step"

def rms_norm(x, w):
    xf = x.astype(jnp.float32)
    y = xf * lax.rsqrt(jnp.mean(xf * xf, axis=-1, keepdims=True) + EPS)
    return (y * w.astype(jnp.float32)).astype(x.dtype)

def chunked_gated_linear(q, k, v, log_a, s0):
    B, L, H, dk = q.shape
    dv = v.shape[-1]
    c = math.gcd(L, CHUNK)
    n = L // c

    def to_chunks(t):
        return t.astype(jnp.float32).reshape(B, n, c, H, t.shape[-1]).transpose(1, 0, 3, 2, 4)

    causal = jnp.tril(jnp.ones((c, c), dtype=bool))[None, None, :, :, None]

    def step(S, inp):
        qc, kc, vc, gc = inp
        b = jnp.cumsum(gc, axis=2)
        o_inter = jnp.einsum('bhtk,bhkv->bhtv', qc * jnp.exp(b), S)
        diff = b[:, :, :, None, :] - b[:, :, None, :, :]
        decay = jnp.where(causal, jnp.exp(jnp.where(causal, diff, 0.0)), 0.0)
        scores = jnp.einsum('bhtk,bhsk,bhtsk->bhts', qc, kc, decay)
        o = o_inter + jnp.einsum('bhts,bhsv->bhtv', scores, vc)
        b_last = b[:, :, -1:, :]
        S_new = jnp.exp(b_last[:, :, 0, :])[..., None] * S + jnp.einsum(
            'bhsk,bhsv->bhkv', kc * jnp.exp(b_last - b), vc)
        return S_new, o

    S_fin, o = lax.scan(step, s0.astype(jnp.float32),
                        (to_chunks(q), to_chunks(k), to_chunks(v), to_chunks(log_a)))
    o = o.transpose(1, 0, 3, 2, 4).reshape(B, L, H, dv)
    return o, S_fin

def head_norm_gate(o, w, gate):
    y = o * lax.rsqrt(jnp.mean(o * o, axis=-1, keepdims=True) + EPS) * w.astype(jnp.float32)
    B, L, H, d = o.shape
    g = jax.nn.silu(gate.astype(jnp.float32)).reshape(B, L, H, d)
    return (y * g).reshape(B, L, H * d)

def token_mix(h, w_in_l, w_lr2_l, b_lr_l, gla_onorm_l, log_lb_l, log1m_lb_l,
              hgrn_onorm_l, w_out_l, s_gla, s_hg):
    B, L, _ = h.shape
    split_points = [int(p) for p in np.cumsum(SPLIT_SIZES)[:-1]]
    proj = h @ w_in_l
    (gq, gk, gv, gg, glr, hq, hf, hi, hg, ga, gb) = jnp.split(proj, split_points, axis=-1)

    q = gq.reshape(B, L, GLA_HEADS, GLA_DK) * (GLA_DK ** -0.5)
    k = gk.reshape(B, L, GLA_HEADS, GLA_DK)
    v = gv.reshape(B, L, GLA_HEADS, GLA_DV)
    log_a = jax.nn.log_sigmoid((glr @ w_lr2_l + b_lr_l).astype(jnp.float32)) / GLA_TAU
    log_a = log_a.reshape(B, L, GLA_HEADS, GLA_DK)
    o_gla, s_gla_new = chunked_gated_linear(q, k, v, log_a, s_gla)
    o_gla = head_norm_gate(o_gla, gla_onorm_l, gg)

    z = hf.astype(jnp.float32)
    log_f = jnp.logaddexp(log_lb_l, log1m_lb_l + jax.nn.log_sigmoid(z))
    key = jnp.exp(log1m_lb_l + jax.nn.log_sigmoid(-z))
    q2 = hq.reshape(B, L, HGRN_HEADS, HGRN_EXPAND)
    k2 = key.reshape(B, L, HGRN_HEADS, HGRN_EXPAND)
    lf = log_f.reshape(B, L, HGRN_HEADS, HGRN_EXPAND)
    v2 = hi.reshape(B, L, HGRN_HEADS, HGRN_DV)
    o_hg, s_hg_new = chunked_gated_linear(q2, k2, v2, lf, s_hg)
    o_hg = head_norm_gate(o_hg, hgrn_onorm_l, hg)

    merged = (jax.nn.sigmoid(ga.astype(jnp.float32)) * o_gla
              + jax.nn.sigmoid(gb.astype(jnp.float32)) * o_hg).astype(h.dtype)
    return merged @ w_out_l, s_gla_new, s_hg_new

def swiglu(h, w_ffn_in_l, w_ffn_out_l):
    a, u = jnp.split(h @ w_ffn_in_l, 2, axis=-1)
    return (jax.nn.silu(a) * u) @ w_ffn_out_l

def setup_inputs(seed: int = 0) -> dict:
    key = jax.random.key(seed)
    ks = jax.random.split(key, 16)
    f32 = jnp.float32
    nrm = lambda k, s, sc: jax.random.normal(k, s, f32) * sc
    gain = lambda k, s: 1.0 + 0.05 * jax.random.normal(k, s, f32)
    return {
        "x_prompt": nrm(ks[0], (BATCH, SEQ, D_MODEL), 1.0),
        "x_sample": nrm(ks[1], (DEC_BATCH, DEC_SEQ, D_MODEL), 1.0),
        "state_gla": nrm(ks[2], (DEPTH, DEC_BATCH, GLA_HEADS, GLA_DK, GLA_DV), 0.5),
        "state_hgrn": nrm(ks[3], (DEPTH, DEC_BATCH, HGRN_HEADS, HGRN_EXPAND, HGRN_DV), 0.5),
        "norm_mix_pre": gain(ks[4], (DEPTH, D_MODEL)),
        "norm_mix_post": gain(ks[5], (DEPTH, D_MODEL)),
        "norm_ffn_pre": gain(ks[6], (DEPTH, D_MODEL)),
        "norm_ffn_post": gain(ks[7], (DEPTH, D_MODEL)),
        "w_in": nrm(ks[8], (DEPTH, D_MODEL, D_IN), D_MODEL ** -0.5),
        "gla_w_lr2": nrm(ks[9], (DEPTH, GLA_GATE_RANK, GLA_HEADS * GLA_DK), GLA_GATE_RANK ** -0.5),
        "gla_b_lr": nrm(ks[10], (DEPTH, GLA_HEADS * GLA_DK), 0.1),
        "gla_onorm": gain(ks[11], (DEPTH, GLA_DV)),
        "hgrn_lb": nrm(ks[12], (DEPTH, HGRN_HEADS * HGRN_EXPAND), 0.5),
        "hgrn_onorm": gain(ks[13], (DEPTH, HGRN_DV)),
        "w_out": nrm(ks[14], (DEPTH, D_MODEL, D_MODEL), D_MODEL ** -0.5),
        "w_ffn_in": nrm(jax.random.fold_in(ks[15], 0), (DEPTH, D_MODEL, 2 * D_FF), D_MODEL ** -0.5),
        "w_ffn_out": nrm(jax.random.fold_in(ks[15], 1), (DEPTH, D_FF, D_MODEL), D_FF ** -0.5),
    }

def reference(x_prompt, x_sample, state_gla, state_hgrn, norm_mix_pre, norm_mix_post,
              norm_ffn_pre, norm_ffn_post, w_in, gla_w_lr2, gla_b_lr, gla_onorm,
              hgrn_lb, hgrn_onorm, w_out, w_ffn_in, w_ffn_out):
    sm = jax.nn.softmax(hgrn_lb.astype(jnp.float32), axis=0)
    lb = jnp.cumsum(sm, axis=0) - sm[0:1]
    lb = jnp.clip(lb, 0.0, 1.0 - 1e-6)
    log_lb = jnp.log(jnp.maximum(lb, LB_FLOOR))
    log1m_lb = jnp.log1p(-lb)

    B = x_prompt.shape[0]
    zero_gla = jnp.zeros((B, GLA_HEADS, GLA_DK, GLA_DV), jnp.float32)
    zero_hg = jnp.zeros((B, HGRN_HEADS, HGRN_EXPAND, HGRN_DV), jnp.float32)

    xp, xs = x_prompt, x_sample
    gla_p, gla_s, hg_p, hg_s = [], [], [], []
    for l in range(DEPTH):
        def layer(x, s_gla, s_hg):
            m, s_gla_new, s_hg_new = token_mix(
                rms_norm(x, norm_mix_pre[l]), w_in[l], gla_w_lr2[l], gla_b_lr[l],
                gla_onorm[l], log_lb[l], log1m_lb[l], hgrn_onorm[l], w_out[l], s_gla, s_hg)
            h = x + rms_norm(m, norm_mix_post[l])
            f = swiglu(rms_norm(h, norm_ffn_pre[l]), w_ffn_in[l], w_ffn_out[l])
            return h + rms_norm(f, norm_ffn_post[l]), s_gla_new, s_hg_new

        xp, sgp, shp = layer(xp, zero_gla, zero_hg)
        xs, sgs, shs = layer(xs, state_gla[l], state_hgrn[l])
        gla_p.append(sgp); gla_s.append(sgs); hg_p.append(shp); hg_s.append(shs)

    return (xp, xs, jnp.stack(gla_p), jnp.stack(gla_s), jnp.stack(hg_p), jnp.stack(hg_s))


_drawn_inputs = setup_inputs


def setup_inputs(seed=0):
    import zlib

    import numpy as np

    out = dict(_drawn_inputs(seed))
    spreads = {}
    factors = {}
    for name, (base, spread) in spreads.items():
        noise = np.random.default_rng([zlib.crc32(name.encode()), seed]).standard_normal(out[name].shape)
        drawn = base * np.exp(spread * noise) if base else spread * noise
        out[name] = __import__('jax').numpy.asarray(drawn.astype(out[name].dtype))
    for name, factor in factors.items():
        out[name] = (out[name] * factor).astype(out[name].dtype)
    return out
```

```python
from contextlib import ExitStack

import concourse.bass as bass
import concourse.mybir as mybir

ALU = mybir.AluOpType
ACT = mybir.ActivationFunctionType
F32 = mybir.dt.float32
F32R = mybir.dt.float32r
I32 = mybir.dt.int32

P = 128
D = 1024
KT = D // P
TP, NB, SL = 512, 8, 8
TS = NB * SL
T = TP + TS
HT = T // 2
C = 128
NC = TP // C
NT = NC + 1
GH, HH = 4, 8
GR, DVG = 16, 256
FF = 2816
FT = FF // P
EPS = 1e-6
TAU = 16.0
LEVELS = (64, 32, 16, 8, 4, 2, 1)
NL = len(LEVELS)
G = GH
ENDS = [0]
for _w in (512, 512, 1024, 1024, GR, 1024, 1024, 1024, 1024, 1024, 1024):
    ENDS.append(ENDS[-1] + _w)
GQ, GK, GV, GG, GLR, HQ, HF, HI, HG, GA, GB = ENDS[:-1]

UNITS = [(HF, 256, 0), (HF, 256, 1), (GK, 128, 0), (GQ, 128, 0), (HQ, 256, 0), (HQ, 256, 1),
         (GV, 256, 0), (GV, 256, 1), (HI, 256, 0), (HI, 256, 1),
         (GA, 256, 0), (GG, 256, 0), (GA, 256, 1), (GG, 256, 1),
         (GB, 256, 0), (HG, 256, 0), (GB, 256, 1), (HG, 256, 1)]
NU = len(UNITS)
GATE0 = 10
UB = 1 + G * NU
UC = UB + D // P
UD = UC + 2 * FT
KCUT = ((0, 8), (8, 8), (16, 6))
NRAW, NSPL = 2, 3

STEPS = (["decay"] + [f"v{i}" for i in range(4)] + ["diag0", "diag1"] + [f"level{i}" for i in range(NL)]
         + ["kt0", "kt1", "diag2", "ds0", "ds1"] + [f"o{i}" for i in range(4)]
         + [f"ss{i}" for i in range(4)] + ["norm0", "norm1", "norm2"])
NR = len(STEPS)
STEP = {name: r for r, name in enumerate(STEPS)}
AFTER = {1: ["decay"], 7: ["v0"], 8: ["v1", "diag0"], 9: ["v2", "diag1", "diag2", "level0"], 10: ["v3", "level1"], 12: ["level2"],
         13: ["level3"], 14: ["level4"], 15: ["level5"], 16: ["level6"],
         17: ["kt0", "kt1", "ds0", "ds1", "o0", "o1", "o2", "o3", "norm0", "norm1", "norm2",
              "ss0", "ss1", "ss2", "ss3"]}
ORDER = [s for n in range(NU) for s in AFTER.get(n, [])]
STEPS = ORDER
STEP = {name: r for r, name in enumerate(STEPS)}
assert len(STEPS) == NR and NR % 2 == 0


def build(nc, x_prompt, x_sample, state_gla, state_hgrn, norm_mix_pre, norm_mix_post, norm_ffn_pre,
          norm_ffn_post, w_in, gla_w_lr2, gla_b_lr, gla_onorm, hgrn_lb, hgrn_onorm, w_out, w_ffn_in,
          w_ffn_out, y_prompt, y_sample, gla_prompt, gla_sample, hgrn_prompt, hgrn_sample):
    keep = ExitStack()

    def sb(name, shape, dt=F32, on=None):
        return (on or keep).enter_context(nc.sbuf_tensor(name, shape, dt))

    def sem(name):
        return keep.enter_context(nc.semaphore(name))

    x_hi = sb("x_hi", [P, KT, T], F32R)
    x_lo = sb("x_lo", [P, KT, T], F32R)
    w_raw_t = sb("w_raw_t", [P, NRAW, KT, P])
    w_hi_t = sb("w_hi_t", [P, NSPL, KT, P], F32R)
    w_lo_t = sb("w_lo_t", [P, NSPL, KT, P], F32R)
    ident = sb("ident", [P, P])
    eps_c = sb("eps_c", [P, 1])
    one_c = sb("one_c", [P, 1])
    gain = sb("gain", [P, 3, KT])
    stat = sb("stat", [P, 2, NT])
    h_t = sb("h_t", [P, NT, D])
    ps = keep.enter_context(nc.psum_tensor("ps", [P, 8, 512], F32))

    def proj(u):
        return ps[:, 2 * (u % 2):2 * (u % 2) + 2, 0:HT]

    def slot(r):
        return ps[:, 4 + 2 * (r % 2):6 + 2 * (r % 2), :].rearrange("p a b -> p (a b)")

    def halves(ap):
        return ap.rearrange("p (a b) -> p a b", a=2)

    w_raw = [sem(f"w_raw{i}") for i in range(NRAW)]
    w_hi = sem("w_hi")
    w_lo = sem("w_lo")
    unit_done = sem("unit_done")
    unit_free = sem("unit_free")
    step_done = sem("step_done")
    step_free = [sem("step_free0"), sem("step_free1")]
    small = sem("small")
    consts = sem("consts")
    setup = sem("setup")
    x_in = sem("x_in")
    squared = sem("squared")
    scaled = sem("scaled")
    turned = sem("turned")
    x_hi_s = sem("x_hi_s")
    x_lo_s = sem("x_lo_s")
    lb_a = sem("lb_a")
    lb_d = sem("lb_d")
    grp_in = sem("grp_in")
    st_in = sem("st_in")
    st_out = sem("st_out")
    lbj_s = sem("lbj_s")
    z_abs = sem("z_abs")
    l_dve = sem("l_dve")
    l2_act = sem("l2_act")
    cum = sem("cum")
    qk_in = sem("qk_in")
    diff = sem("diff")
    expd = sem("expd")
    lvl = sem("lvl")
    qs = sem("qs")
    dec_s = sem("dec_s")
    a_s = sem("a_s")
    v_in = sem("v_in")
    v_tok = sem("v_tok")
    k_tok = sem("k_tok")
    sp_s = sem("sp_s")
    kblk_s = sem("kblk_s")
    ss_s = sem("ss_s")
    gate_in = sem("gate_in")
    gate_s = sem("gate_s")
    o_sq = sem("o_sq")
    rst = sem("rst")
    merged_s = sem("merged_s")
    glr_s = sem("glr_s")

    v2 = lambda w: w.rearrange("o (k p) n -> p (o k) n", p=P)
    win_v, wout_v, wf1_v, wf2_v = v2(w_in), v2(w_out), v2(w_ffn_in), v2(w_ffn_out)
    xp_v = x_prompt.rearrange("o (c p) d -> c p (o d)", p=P)
    xs_v = x_sample.rearrange("b t d -> (b t) d")
    yp_v = y_prompt.rearrange("o (c p) d -> c p (o d)", p=P)
    ys_v = y_sample.rearrange("b t d -> (b t) d")
    tok = lambda c: P if c < NC else TS

    def held(eng, scratch, s, value):
        eng.wait_ge(s, value)
        eng.reg_alu(scratch, scratch, 1, ALU.add)

    def load_unit(eng, u, src, nk=KT):
        eng.dma_start(w_raw_t[:, u % NRAW, 0:nk, :], src).then_inc(w_raw[u % NRAW], 16)

    def loaded(u, more=0):
        return more * 16 + 16 * (u // NRAW + 1)

    def split_hi(u, nk=KT):
        nc.scalar.activation(w_hi_t[:, u % NSPL, 0:nk, :], w_raw_t[:, u % NRAW, 0:nk, :],
                             ACT.Copy).then_inc(w_hi, 1)

    def split_lo(u, nk=KT):
        nc.vector.tensor_tensor(w_lo_t[:, u % NSPL, 0:nk, :], w_raw_t[:, u % NRAW, 0:nk, :],
                                w_hi_t[:, u % NSPL, 0:nk, :].bitcast(F32), ALU.subtract).then_inc(w_lo, 1)

    def unit_passes(u, out, hi, lo, nk=KT, first=True, last=True):
        todo = [(w, x, k) for k in range(nk) for w, x in ((w_lo_t, hi), (w_hi_t, lo), (w_hi_t, hi))]
        for i, (w, x, k) in enumerate(todo):
            for q in range(2):
                m = nc.tensor.matmul(out[:, q, :], w[:, u % NSPL, k, :], x(k, q),
                                     start=first and i == 0, stop=last and i == len(todo) - 1)
        return m

    xh = lambda k, q: x_hi[:, k, q * HT:(q + 1) * HT]
    xl = lambda k, q: x_lo[:, k, q * HT:(q + 1) * HT]

    merged_stack = ExitStack()
    merged = sb("merged", [P, KT, T], F32, merged_stack)
    sa = ExitStack()
    A = lambda name, shape, dt=F32: sb(name, shape, dt, sa)
    Z = A("Z", [P, 3, T])
    L4 = A("L4", [P, 4, T])
    T3 = A("T3", [P, 3, T])
    B = A("B", [P, 3, T])
    Q = A("Q", [P, 3, T])
    K = A("K", [P, 3, T])
    Am = A("Am", [P, NC * 3, C])
    As = A("As", [TS, 3, TS])
    v_t = A("v_t", [P, NT, 4 * P])
    k_t = A("k_t", [P, NT, 3 * P])
    sp_t = A("sp_t", [P, NC, 4 * P])
    ssg = h_t[:, 0:2, :].rearrange("p a (b v) -> p (a b) v", v=DVG)
    ssh = h_t[:, 2:4, :].rearrange("p a (b h v) -> p (a b) h v", h=2, v=P)
    Gt = A("Gt", [P, 4, T])
    E2 = A("E2", [P, 2, T])
    glr = A("glr", [GR, T])
    wlr = A("wlr", [GR, P])
    blr4 = A("blr4", [P, GH])
    blr = A("blr", [P, 1])
    ones = A("ones", [P, P])
    mask = A("mask", [P, NL, C // 2])
    seg = A("seg", [P, T])
    rowm = A("rowm", [TS, NB])
    tick = A("tick", [1, 1])
    pool_w = A("pool_w", [1, 2])
    onm = A("onm", [P, 3])
    lb = A("lb", [P, 6, HH])
    lbj = A("lbj", [P, 3, 2])
    dec = A("dec", [P, 3, NC + NB])
    k_flat = k_t[:, :, :].rearrange("p a b -> p (a b)")
    kblk = T3[:, :, :].rearrange("p a b -> p (a b)")[0:TS, 0:NB * P].rearrange("p (b d) -> p b d", b=NB)
    xt = [h_t[:, c, :] for c in range(NT)]
    square = v_t[:, :, :].rearrange("p a b -> p (a b)")[:, 0:D]
    sqo = [Z[:, 0, :], Z[:, 1, :], Z[:, 2, :], T3[:, 2, :]]
    head_of = (0, 0, 1, 2)

    def second(ap, L):
        return ap.rearrange("p (n b) -> p n b", b=2 * L)[:, :, L:2 * L]

    block = nc.Block()
    with block:
        @block.sync
        def _(sp):
            for c in range(NT):
                sp.dma_start(xt[c][0:tok(c), :], xp_v[c] if c < NC else xs_v).then_inc(x_in, 16)
            for t, v in ((gain[:, 0, :], norm_mix_pre), (gain[:, 1, :], norm_ffn_pre), (gain[:, 2, :], hgrn_lb),
                         (onm[:, 0:2], gla_onorm), (onm[:, 2:3], hgrn_onorm), (blr4[:, :], gla_b_lr)):
                sp.dma_start(t, v).then_inc(small, 16)
            load_unit(sp, 0, win_v[:, :, GLR:GLR + P])
            with nc.sync.Fori(0, G) as j:
                j18 = sp.snap(j * NU)
                for n, (col, width, t) in enumerate(UNITS):
                    first = (j * (width // P) + (col // P + t)) * P + col % P
                    sp.wait_ge(w_lo, j18 + (n + 1))
                    load_unit(sp, n + 1, win_v[:, :, bass.ds(first, P)])
            for u in range(UB, UB + 2):
                sp.wait_ge(w_lo, u)
                load_unit(sp, u, wout_v[:, :, (u - UB) * P:(u - UB + 1) * P])
            sp.wait_ge(w_lo, UB + 2)

        @block.gpsimd
        def _(pool):
            n = 0

            def hold(s, value):
                pool.wait_ge(s, value)
                nc.gpsimd.tensor_tensor(pool_w[:, 1:2], pool_w[:, 0:1], pool_w[:, 0:1], ALU.add)
                pool.drain()
            for t in (ident, ones, seg, mask, rowm, pool_w):
                ins = nc.gpsimd.memset(t[:], 0.0 if t is ident else 1.0)
                ins.then_inc(consts, 1)
                n += 1
            pool.wait_ge(consts, n)
            nc.gpsimd.affine_select(out=ident[:], in_=ident[:], compare_op=ALU.not_equal, fill=1.0, base=0,
                                    pattern=[[-1, P]], channel_multiplier=1).then_inc(consts, 1)
            nc.gpsimd.memset(seg[:, 0:TP].rearrange("p (c t) -> p c t", t=C)[:, :, 0:1], 0.0).then_inc(consts, 1)
            nc.gpsimd.memset(seg[:, TP:T].rearrange("p (c t) -> p c t", t=SL)[:, :, 0:1], 0.0).then_inc(consts, 1)
            n += 3
            for i, L in enumerate(LEVELS):
                m = mask[:, i, :].rearrange("p (a r) -> p a r", r=L)
                nc.gpsimd.affine_select(out=m, in_=m, compare_op=ALU.is_ge, fill=0.0, base=0,
                                        pattern=[[-2 * L, C // 2 // L], [0, L]], channel_multiplier=1).then_inc(consts, 1)
                n += 1
                pool.wait_ge(consts, n)
                nc.gpsimd.affine_select(out=m, in_=m, compare_op=ALU.is_ge, fill=0.0, base=L - 1,
                                        pattern=[[2 * L, C // 2 // L], [0, L]], channel_multiplier=-1).then_inc(consts, 1)
                n += 1
            nc.gpsimd.affine_select(out=rowm[:], in_=rowm[:], compare_op=ALU.is_ge, fill=0.0, base=0,
                                    pattern=[[-SL, NB]], channel_multiplier=1).then_inc(consts, 1)
            n += 1
            pool.wait_ge(consts, n)
            nc.gpsimd.affine_select(out=rowm[:], in_=rowm[:], compare_op=ALU.is_ge, fill=0.0, base=SL - 1,
                                    pattern=[[SL, NB]], channel_multiplier=-1).then_inc(consts, 1)
            n += 1
            assert n == CONSTS, n
            pool.wait_ge(turned, KT)
            with nc.gpsimd.Fori(0, G) as j:
                pool.dma_start(wlr[:, :], gla_w_lr2[0, :, bass.ds(j * P, P)]).then_inc(grp_in, 16)
                pool.dma_start(ssg[:, :, :], state_gla.rearrange("o b h k v -> k (o b h) v").rearrange(
                    "k (b h) v -> k h b v", h=GH)[:, bass.ds(j, 1), :, :].rearrange("k o b v -> k (o b) v")).then_inc(st_in, 16)
                for i in range(2):
                    pool.dma_start(ssh[:, :, i, :], state_hgrn.rearrange("o b h k v -> k (o b h) v").rearrange(
                        "k (b h) v -> k h b v", h=HH)[:, bass.ds(2 * j + i, 1), :, :].rearrange("k o b v -> k (o b) v")).then_inc(st_in, 16)
                hold(sp_s, j * 2 + 2)
                pool.dma_start(gla_prompt.rearrange("o b h k v -> k (o b h) v")[:, bass.ds(j, 1), :],
                               sp_t[:, NC - 1:NC, 0:DVG]).then_inc(st_out, 16)
                pool.dma_start(hgrn_prompt.rearrange("o b h k v -> k (o b h) v")[:, bass.ds(2 * j, 2), :],
                               sp_t[:, NC - 1, DVG:2 * DVG].rearrange("k (h v) -> k h v", h=2)).then_inc(st_out, 16)
                hold(ss_s, j * 4 + 4)
                pool.dma_start(gla_sample.rearrange("o b h k v -> k (o b h) v").rearrange(
                    "k (b h) v -> k h b v", h=GH)[:, bass.ds(j, 1), :, :].rearrange("k o b v -> k (o b) v"), ssg[:, :, :]).then_inc(st_out, 16)
                for i in range(2):
                    pool.dma_start(hgrn_sample.rearrange("o b h k v -> k (o b h) v").rearrange(
                        "k (b h) v -> k h b v", h=HH)[:, bass.ds(2 * j + i, 1), :, :].rearrange("k o b v -> k (o b) v"), ssh[:, :, i, :]).then_inc(st_out, 16)
                hold(st_out, j * 80 + 80)

        @block.scalar
        def _(act):
            scratch = act.alloc_register("act_scratch")
            act.reg_mov(scratch, 0)
            act.preload_act_table_set("natural_log_exp_and_others")
            act.wait_ge(setup, SETUP)
            for c in range(NT):
                act.wait_ge(x_in, 16 * NT)
                act.activation(square[0:tok(c), :], xt[c][0:tok(c), :], ACT.Square, accum_out=stat[0:tok(c), 0, c:c + 1])
                act.drain()
            act.activation(stat[:, 1, :], stat[:, 0, :], ACT.Ln, scale=1.0 / D, bias=eps_c[:, :])
            act.drain()
            act.activation(stat[:, 1, :], stat[:, 1, :], ACT.Exp, scale=-0.5).then_inc(squared, 1)
            act.wait_ge(lb_d, 1)
            act.activation(lb[:, 1, :], lb[:, 1, :], ACT.Exp).then_inc(lb_a, 1)
            act.wait_ge(lb_d, 2)
            act.activation(lb[:, 4, :], lb[:, 4, :], ACT.Ln)
            act.activation(lb[:, 5, :], lb[:, 5, :], ACT.Ln, scale=-1.0, bias=one_c[:, :]).then_inc(lb_a, 1)
            for k in range(KT):
                act.wait_ge(turned, k + 1)
                act.activation(x_hi[:, k, :], turn_slot(ps, k)[:, 0:T], ACT.Copy, scale=gain[:, 0, k:k + 1]).then_inc(x_hi_s, 1)
            for u in range(3):
                act.wait_ge(w_raw[u % NRAW], loaded(u))
                split_hi(u)
            act.wait_ge(unit_done, 1)
            act.activation(halves(glr[:, :]), proj(0)[0:GR], ACT.Copy).then_inc(unit_free, 1)
            with nc.scalar.Fori(0, G) as j:
                j18 = act.snap(j * NU)
                jr = act.snap(j * NR)
                hold = lambda s, v: held(act, scratch, s, v)

                def step(name):
                    hold(step_done, jr + (STEP[name] + 1))

                def freed(ins, name):
                    ins.then_inc(step_free[STEP[name] % 2], 1)

                def evacuate(n):
                    hold(unit_done, j18 + (n + 2))
                    src = proj(n + 1)
                    if n < 2:
                        act.activation(halves(Z[:, 1 + n, :]), src, ACT.Copy).then_inc(unit_free, 1)
                    elif n == 2:
                        act.activation(halves(K[:, 0, :]), src, ACT.Copy).then_inc(unit_free, 1)
                    elif n < 6:
                        act.activation(halves(Q[:, n - 3, :]), src, ACT.Copy,
                                       scale=float(P) ** -0.5 if n == 3 else 1.0).then_inc(unit_free, 1)
                    elif n < GATE0:
                        if n == 6:
                            hold(merged_s, j + 1)
                        act.activation(halves(Gt[:, n - 6, :]), src, ACT.Copy).then_inc(unit_free, 1)
                    elif n % 2 == 0:
                        hold(gate_s, j * 4 + ((n - GATE0) // 2 + 1))
                        act.activation(halves(E2[:, 0, :]), src, ACT.Exp, scale=-1.0).then_inc(unit_free, 1)
                    else:
                        act.activation(halves(E2[:, 1, :]), src, ACT.Exp, scale=-1.0)
                        act.activation(halves(Gt[:, (n - GATE0) // 2, :]), src, ACT.Copy).then_inc(unit_free, 1)

                def level_exp(i):
                    hold(diff, j * (NL + 1) + (i + 1))
                    L = LEVELS[i]
                    z = Z[:, :, 0:TP] if L > 4 else Z[:, :, :]
                    z = z.rearrange("p h (n b) -> p h n b", b=2 * L)
                    if L <= 4:
                        z = Z[:, :, :].rearrange("p h (n b) -> p (h n) b", b=2 * L)
                        act.activation(z[:, :, 0:L], z[:, :, 0:L], ACT.Exp, scale=-1.0)
                        act.activation(z[:, :, L:2 * L], z[:, :, L:2 * L], ACT.Exp).then_inc(expd, 1)
                    else:
                        act.activation(z[:, :, :, 0:L], z[:, :, :, 0:L], ACT.Exp, scale=-1.0)
                        act.activation(z[:, :, :, L:2 * L], z[:, :, :, L:2 * L], ACT.Exp).then_inc(expd, 1)

                def turn_v(d):
                    step(f"v{d}")
                    s = slot(STEP[f"v{d}"])
                    act.activation(v_t[:, 0:NC, d * P:(d + 1) * P], s[:, 0:TP].rearrange("p (c v) -> p c v", c=NC), ACT.Copy)
                    ins = act.activation(v_t[0:TS, NC, d * P:(d + 1) * P], s[0:TS, TP:TP + P], ACT.Copy)
                    freed(ins, f"v{d}")

                for n in range(NU):
                    hold(w_raw[(n + 3) % NRAW], loaded(n + 3, j * (NU // NRAW)))
                    hold(unit_done, j18 + (n + 1))
                    split_hi(n + 3)
                    if n >= 1:
                        evacuate(n - 1)
                    if n == 2:
                        hold(lbj_s, j * 4 + 4)
                        step("decay")
                        freed(act.activation(halves(Z[:, 0, :]), slot(STEP["decay"]).rearrange("p (a b) -> p a b", a=2)[:, :, 0:HT],
                                             ACT.Identity, bias=blr[:, :]), "decay")
                        act.drain()
                        act.activation(T3[:, :, :], Z[:, :, :], ACT.Abs)
                        act.drain()
                        act.activation(T3[:, :, :], T3[:, :, :], ACT.Exp, scale=-1.0)
                        act.drain()
                        act.activation(T3[:, :, :], T3[:, :, :], ACT.Ln, bias=one_c[:, :]).then_inc(z_abs, 1)
                    if n == 3:
                        hold(l_dve, j + 1)
                        for h in range(2):
                            act.activation(T3[:, 1 + h, :], L4[:, 1 + h, :], ACT.Abs, bias=lbj[:, 2, h:h + 1])
                            act.activation(K[:, 1 + h, :], K[:, 1 + h, :], ACT.Exp, bias=lbj[:, 0, h:h + 1])
                        act.drain()
                        act.activation(T3[:, 1:3, :], T3[:, 1:3, :], ACT.Exp, scale=-1.0)
                        act.drain()
                        act.activation(T3[:, 1:3, :], T3[:, 1:3, :], ACT.Ln, bias=one_c[:, :]).then_inc(l2_act, 1)
                    if n == 6:
                        act.drain().then_inc(qk_in, 1)
                        level_exp(0)
                    if 8 <= n < 12:
                        turn_v(n - 8)
                    if n in LEVEL_AT and LEVEL_AT[n] > 0:
                        level_exp(LEVEL_AT[n])
                    if 7 <= n <= 10:
                        act.drain().then_inc(v_in, 1)
                    if n > GATE0 and (n - GATE0) % 2 == 0:
                        act.drain().then_inc(gate_in, 1)
                evacuate(NU - 1)
                act.drain().then_inc(gate_in, 1)
                hold(cum, j + 1)
                bl = B[:, :, 0:TP].rearrange("p h (c t) -> p h c t", t=C)[:, :, :, C - 1]
                bs = B[:, :, TP:T].rearrange("p h (c t) -> p h c t", t=SL)[:, :, :, SL - 1]
                hold(lvl, j * NL + NL)
                act.activation(Z[:, :, :], B[:, :, :], ACT.Exp).then_inc(expd, 1)
                act.activation(dec[:, :, 0:NC], bl, ACT.Exp)
                act.activation(dec[:, :, NC:NC + NB], bs, ACT.Exp).then_inc(dec_s, 1)
                hold(diff, j * (NL + 1) + NL + 1)
                act.activation(Z[:, :, :], Z[:, :, :], ACT.Exp).then_inc(expd, 1)
                step("kt0")
                freed(act.activation(k_flat[:, 0:8 * P], slot(STEP["kt0"]), ACT.Copy), "kt0")
                step("kt1")
                act.activation(k_flat[:, 8 * P:12 * P], slot(STEP["kt1"])[:, 0:4 * P], ACT.Copy)
                freed(act.activation(k_flat[0:TS, 12 * P:15 * P], slot(STEP["kt1"])[0:TS, 4 * P:7 * P], ACT.Copy), "kt1")
                act.drain().then_inc(k_tok, 1)
                for d in range(4):
                    step(f"o{d}")
                    act.activation(L4[:, d, :], slot(STEP[f"o{d}"])[:, 0:T], ACT.Copy)
                    freed(act.activation(sqo[d], slot(STEP[f"o{d}"])[:, 0:T], ACT.Square), f"o{d}")
                    act.drain().then_inc(o_sq, 1)
                for h in range(3):
                    step(f"norm{h}")
                    freed(act.activation(B[:, h, :], slot(STEP[f"norm{h}"])[:, 0:T], ACT.Ln,
                                         scale=1.0 / (DVG if h == 0 else P), bias=eps_c[:, :]), f"norm{h}")
                    act.drain()
                    act.activation(B[:, h, :], B[:, h, :], ACT.Exp, scale=-0.5).then_inc(rst, 1)

        @block.vector
        def _(dve):
            dve.memset(eps_c[:, :], EPS)
            dve.memset(one_c[:, :], 1.0)
            dve.memset(stat[:, :, :], 1.0).then_inc(setup, 1)
            dve.drain().then_inc(w_lo, 1)
            dve.drain().then_inc(unit_free, 1)
            dve.drain().then_inc(step_free[0], 1)
            dve.drain().then_inc(step_free[1], 1)
            dve.drain().then_inc(gate_s, 1)
            dve.drain().then_inc(merged_s, 1)
            dve.wait_ge(small, 16 * 6)
            dve.tensor_tensor(lb[:, 1, :], gain[:, 2, :], gain[:, 2, :], ALU.subtract).then_inc(lb_d, 1)
            dve.wait_ge(lb_a, 1)
            dve.reciprocal(lb[:, 2, :], lb[:, 1, :])
            dve.drain()
            dve.tensor_tensor(lb[:, 1, :], lb[:, 1, :], lb[:, 2, :], ALU.mult)
            dve.drain()
            dve.tensor_tensor(lb[:, 3, :], lb[:, 1, :], lb[:, 1, :], ALU.subtract)
            dve.drain()
            dve.tensor_scalar(lb[:, 5, :], lb[:, 3, :], 0.0, 1.0 - 1e-6, ALU.max, ALU.min)
            dve.drain()
            dve.tensor_scalar(lb[:, 4, :], lb[:, 5, :], 1e-20, 2.0 ** 40, ALU.max, ALU.mult).then_inc(lb_d, 1)
            dve.wait_ge(lb_a, 2)
            dve.tensor_scalar(lb[:, 4, :], lb[:, 4, :], -LOG2_40, None, ALU.add)
            dve.drain()
            dve.tensor_tensor(lb[:, 3, :], lb[:, 5, :], lb[:, 4, :], ALU.subtract)
            dve.wait_ge(squared, 1)
            for c in range(NT):
                dve.tensor_scalar(xt[c][0:tok(c), :], xt[c][0:tok(c), :], stat[0:tok(c), 1, c:c + 1], None, ALU.mult).then_inc(scaled, 1)
            for k in range(KT):
                dve.wait_ge(x_hi_s, k + 1)
                dve.scalar_tensor_tensor(x_lo[:, k, :], turn_slot(ps, k)[:, 0:T], gain[:, 0, k:k + 1],
                                         x_hi[:, k, :].bitcast(F32), ALU.mult, ALU.subtract).then_inc(x_lo_s, 1)
            for u in range(3):
                dve.wait_ge(w_hi, u + 1)
                split_lo(u)
            dve.wait_ge(consts, CONSTS)
            with nc.vector.Fori(0, G) as j:
                j18 = dve.snap(j * NU)
                jr = dve.snap(j * NR)

                def step(name):
                    dve.wait_ge(step_done, jr + (STEP[name] + 1))

                def freed(ins, name):
                    ins.then_inc(step_free[STEP[name] % 2], 1)

                def level_view(t, L):
                    if L > 4:
                        return t[:, 0:3, 0:TP].rearrange("p h (n b) -> p h n b", b=2 * L)
                    return t[:, 0:3, :].rearrange("p h (n b) -> p (h n) b", b=2 * L)

                def level_diff(i):
                    L = LEVELS[i]
                    b, z = level_view(B, L), level_view(Z, L)
                    if L > 4:
                        dve.tensor_tensor(z, b, b[:, :, :, L - 1:L].broadcast_to([P, 3, TP // (2 * L), 2 * L]), ALU.subtract).then_inc(diff, 1)
                    else:
                        dve.tensor_tensor(z, b, b[:, :, L - 1:L].broadcast_to([P, 3 * T // (2 * L), 2 * L]), ALU.subtract).then_inc(diff, 1)

                def level_scale(i):
                    dve.wait_ge(expd, j * (NL + 2) + (i + 1))
                    if i == 0:
                        dve.wait_ge(qk_in, j + 1)
                    if i >= 2:
                        step(f"level{i - 2}")
                    L = LEVELS[i]
                    m, z, q, k = (level_view(t, L) for t in ((L4, T3)[i % 2], Z, Q, K))
                    if L > 4:
                        dve.tensor_tensor(m[:, :, :, 0:L], z[:, :, :, 0:L], k[:, :, :, 0:L], ALU.mult)
                        dve.tensor_tensor(m[:, :, :, L:2 * L], z[:, :, :, L:2 * L], q[:, :, :, L:2 * L], ALU.mult).then_inc(lvl, 1)
                    else:
                        dve.tensor_tensor(m[:, :, 0:L], z[:, :, 0:L], k[:, :, 0:L], ALU.mult)
                        dve.tensor_tensor(m[:, :, L:2 * L], z[:, :, L:2 * L], q[:, :, L:2 * L], ALU.mult).then_inc(lvl, 1)
                    dve.drain()

                def level_take(i):
                    dve.drain()
                    step(f"level{i}")
                    dve.memset(tick[:, :], 0.0)
                    L = LEVELS[i]
                    s = slot(STEP[f"level{i}"])
                    n = C // 2 // L
                    m = mask[:, i, :].bitcast(I32).rearrange("p (o a r) -> p o a r", o=1, r=L)
                    ins = dve.copy_predicated(
                        Am[:, :, :].rearrange("p h (a b) -> p h a b", b=2 * L)[:, :, :, L:2 * L],
                        m.broadcast_to([P, 3 * NC, n, L]),
                        s[:, 0:3 * NC * C // 2].rearrange("p (h a r) -> p h a r", a=n, r=L))
                    if L <= 4:
                        n = TS // 2 // L
                        o = 3 * NC * C // 2
                        ins = dve.copy_predicated(
                            As[:, :, :].rearrange("p h (a b) -> p h a b", b=2 * L)[:, :, :, L:2 * L],
                            m[0:TS, :, 0:n, :].broadcast_to([TS, 3, n, L]),
                            s[0:TS, o:o + 3 * TS // 2].rearrange("p (h a r) -> p h a r", a=n, r=L))
                    freed(ins, f"level{i}")

                def diagonal(i):
                    step(f"diag{i}")
                    s = slot(STEP[f"diag{i}"])
                    if i < 2:
                        ins = dve.tensor_tensor(Am[:, 6 * i:6 * i + 6, :], s[:, 0:6 * C].rearrange("p (h t) -> p h t", t=C),
                                                ident[:, :].rearrange("p (o t) -> p o t", o=1).broadcast_to([P, 6, C]), ALU.mult)
                    else:
                        ins = dve.tensor_tensor(As[:, :, :], s[0:TS, 0:3 * TS].rearrange("p (h t) -> p h t", t=TS),
                                                ident[0:TS, 0:TS].rearrange("p (o t) -> p o t", o=1).broadcast_to([TS, 3, TS]), ALU.mult)
                    freed(ins, f"diag{i}")

                def gate(t):
                    dve.wait_ge(gate_in, j * 4 + (t + 1))
                    dve.tensor_scalar(E2[:, 0, :], E2[:, 0, :], 1.0, None, ALU.add)
                    dve.drain()
                    dve.scalar_tensor_tensor(E2[:, 1, :], E2[:, 1, :], 1.0, E2[:, 0, :], ALU.add, ALU.mult)
                    dve.drain()
                    dve.reciprocal(E2[:, 1, :], E2[:, 1, :])
                    dve.drain()
                    dve.tensor_tensor(Gt[:, t, :], Gt[:, t, :], E2[:, 1, :], ALU.mult).then_inc(gate_s, 1)

                dve.tensor_copy(blr[:, :], blr4[:, bass.ds(j, 1)]).then_inc(lbj_s, 1)
                for a, b in ((0, 5), (1, 4), (2, 3)):
                    dve.tensor_copy(lbj[:, a, :], lb[:, b, bass.ds(2 * j, 2)]).then_inc(lbj_s, 1)
                dve.drain()
                for n in range(NU):
                    dve.wait_ge(w_hi, j18 + (n + 4))
                    split_lo(n + 3)
                    if n == 3:
                        dve.wait_ge(z_abs, j + 1)
                        dve.scalar_tensor_tensor(L4[:, 0:3, :], Z[:, :, :], 0.0, T3[:, :, :], ALU.min, ALU.subtract)
                        dve.drain()
                        dve.tensor_tensor(K[:, 1:3, :], L4[:, 1:3, :], Z[:, 1:3, :], ALU.subtract).then_inc(l_dve, 1)
                        dve.tensor_scalar(L4[:, 0, :], L4[:, 0, :], 1.0 / TAU, None, ALU.mult)
                        for h in range(2):
                            dve.tensor_scalar(B[:, 1 + h, :], L4[:, 1 + h, :], lbj[:, 0, h:h + 1], lbj[:, 1, h:h + 1],
                                              ALU.add, ALU.max)
                    if n == 4:
                        dve.drain()
                        dve.wait_ge(l2_act, j + 1)
                        dve.tensor_tensor(L4[:, 1:3, :], B[:, 1:3, :], T3[:, 1:3, :], ALU.add)
                        dve.drain()
                        for h in range(3):
                            ins = dve.tensor_tensor_scan(B[:, h, :], seg[:, :], L4[:, h, :], 0.0, ALU.mult, ALU.add)
                        ins.then_inc(cum, 1)
                        dve.drain()
                        level_diff(0)
                    if n == 7:
                        level_scale(0)
                        level_diff(1)
                    if n == 9:
                        diagonal(0)
                        level_scale(1)
                        level_diff(2)
                    if n == 10:
                        diagonal(1)
                        diagonal(2)
                        level_take(0)
                        level_scale(2)
                        level_diff(3)
                    if n == 12:
                        level_take(1)
                        level_scale(3)
                        gate(0)
                        level_diff(4)
                    if n == 13:
                        level_take(2)
                        level_scale(4)
                        level_diff(5)
                    if n == 14:
                        level_take(3)
                        level_scale(5)
                        gate(1)
                        level_diff(6)
                    if n == 15:
                        level_take(4)
                        level_scale(6)
                    if n == 16:
                        level_take(5)
                        gate(2)
                dve.drain()
                dve.wait_ge(expd, j * (NL + 2) + NL + 1)
                dve.tensor_tensor(Q[:, :, :], Q[:, :, :], Z[:, :, :], ALU.mult).then_inc(qs, 1)
                dve.drain()
                for z, b, n, t in ((Z[:, :, 0:TP], B[:, :, 0:TP], NC, C), (Z[:, :, TP:T], B[:, :, TP:T], NB, SL)):
                    z, b = (a.rearrange("p h (c t) -> p h c t", t=t) for a in (z, b))
                    ins = dve.tensor_tensor(z, b[:, :, :, t - 1:t].broadcast_to([P, 3, n, t]), b, ALU.subtract)
                ins.then_inc(diff, 1)
                dve.wait_ge(expd, j * (NL + 2) + NL + 2)
                dve.tensor_tensor(K[:, :, :], K[:, :, :], Z[:, :, :], ALU.mult).then_inc(qs, 1)
                level_take(6)
                dve.drain().then_inc(a_s, 1)
                gate(3)
                dve.drain()
                dve.wait_ge(dec_s, j + 1)
                for i in range(2):
                    if i:
                        dve.drain()
                    step(f"ds{i}")
                    s = slot(STEP[f"ds{i}"])
                    for c in (2 * i, 2 * i + 1):
                        dS = s[:, (c % 2) * 4 * P:(c % 2 + 1) * 4 * P]
                        if c == 0:
                            ins = dve.tensor_copy(sp_t[:, 0, :], dS)
                        else:
                            if c != 2:
                                dve.drain()
                            for h, (a, b) in enumerate(((0, 256), (256, 384), (384, 512))):
                                ins = dve.scalar_tensor_tensor(sp_t[:, c, a:b], sp_t[:, c - 1, a:b], dec[:, h, c:c + 1],
                                                               dS[:, a:b], ALU.mult, ALU.add)
                    freed(ins, f"ds{i}")
                    dve.drain().then_inc(sp_s, 1)
                for h in range(3):
                    dve.wait_ge(rst, j * 3 + (h + 1))
                    for d in ((0, 1), (2,), (3,))[h]:
                        dve.scalar_tensor_tensor(L4[:, d, :], L4[:, d, :], onm[:, min(d, 2):min(d, 2) + 1], B[:, h, :], ALU.mult, ALU.mult)
                        dve.drain()
                        dve.tensor_tensor(L4[:, d, :], L4[:, d, :], Gt[:, d, :], ALU.mult)
                dve.drain()
                dve.tensor_tensor(merged[:, bass.ds(2 * j, 2), :], L4[:, 0:2, :], L4[:, 2:4, :], ALU.add).then_inc(merged_s, 1)
                for i in range(4):
                    h = (0, 0, 1, 2)[i]
                    if i != 1:
                        if i > 0:
                            step(f"ss{i - 1}")
                        dve.wait_ge(k_tok, j + 1)
                        dve.tensor_tensor(kblk, k_t[0:TS, NC:NC + 1, h * P:(h + 1) * P].broadcast_to([TS, NB, P]),
                                          rowm[:, :].rearrange("p (b o) -> p b o", o=1).broadcast_to([TS, NB, P]), ALU.mult).then_inc(kblk_s, 1)
                    if i < 2:
                        st, b0, nb, w = ssg[:, 4 * i:4 * i + 4, :], 4 * i, 4, DVG
                    else:
                        st, b0, nb, w = ssh[:, :, i - 2, :], 0, NB, P
                    dve.wait_ge(step_done, jr + (STEP["norm2"] + 1))
                    dve.tensor_tensor(st, st, dec[:, h, NC + b0:NC + b0 + nb].rearrange("p (b o) -> p b o", o=1).broadcast_to([P, nb, w]), ALU.mult)
                    dve.drain()
                    step(f"ss{i}")
                    ins = dve.tensor_tensor(st, st, slot(STEP[f"ss{i}"])[:, 0:nb * w].rearrange("p (b v) -> p b v", b=nb), ALU.add)
                    freed(ins, f"ss{i}")
                    dve.drain().then_inc(ss_s, 1)

        @block.tensor
        def _(pe):
            pe.wait_ge(consts, CONSTS)
            for k in range(KT):
                if k >= 4:
                    pe.wait_ge(x_lo_s, k - 3)
                for c in range(NT):
                    if k == 0:
                        pe.wait_ge(scaled, c + 1)
                    m = nc.tensor.transpose(turn_slot(ps, k)[:, c * P:c * P + tok(c)], xt[c][0:tok(c), k * P:(k + 1) * P],
                                            ident[0:tok(c), 0:tok(c)])
                m.then_inc(turned, 1)
            pe.wait_ge(x_lo_s, KT)
            pe.wait_ge(w_lo, 2)
            unit_passes(0, proj(0), xh, xl).then_inc(unit_done, 1)
            pe.wait_ge(unit_free, 2)
            with nc.tensor.Fori(0, G) as j:
                j18 = pe.snap(j * NU)
                jh = pe.snap(j * (NR // 2))

                def taken(name):
                    pe.wait_ge(step_free[STEP[name] % 2], jh + (STEP[name] // 2 + 1))

                def do_step(name):
                    r = STEP[name]
                    s = slot(r)
                    taken(name)
                    if name == "decay":
                        pe.wait_ge(grp_in, j * 16 + 16)
                        for q in range(2):
                            m = nc.tensor.matmul(s[:, q * 512:q * 512 + HT], wlr[:, :], glr[:, q * HT:(q + 1) * HT], start=True, stop=True)
                    elif name[0] == "v":
                        d = int(name[1:])
                        pe.wait_ge(v_in, j * 4 + (d + 1))
                        for c in range(NT):
                            m = nc.tensor.transpose(s[0:tok(c), c * P:(c + 1) * P], Gt[:, d, c * P:c * P + tok(c)], ident[:, :])
                    elif name[:4] == "diag":
                        i = int(name[4:])
                        if i == 0:
                            pe.wait_ge(qk_in, j + 1)
                        for a in range(6 if i < 2 else 0):
                            c, h = divmod(6 * i + a, 3)
                            m = nc.tensor.matmul(s[:, a * C:(a + 1) * C], K[:, h, c * C:(c + 1) * C], Q[:, h, c * C:(c + 1) * C],
                                                 start=True, stop=True)
                        if i == 2:
                            for h in range(3):
                                m = nc.tensor.matmul(s[0:TS, h * TS:(h + 1) * TS], K[:, h, TP:T], Q[:, h, TP:T],
                                                     start=True, stop=True)
                    elif name[:5] == "level":
                        i = int(name[5:])
                        L = LEVELS[i]
                        M = (L4, T3)[i % 2]
                        pe.wait_ge(lvl, j * NL + (i + 1))
                        for a in range(3 * NC):
                            c, h = divmod(a, 3)
                            w = M[:, h, c * C:(c + 1) * C]
                            m = nc.tensor.matmul(s[:, a * C // 2:(a + 1) * C // 2], w, second(w, L), start=True, stop=True)
                        if L <= 4:
                            for h in range(3):
                                w = M[:, h, TP:T]
                                o = 3 * NC * C // 2 + h * TS // 2
                                m = nc.tensor.matmul(s[0:TS, o:o + TS // 2], w, second(w, L), start=True, stop=True)
                    elif name[:2] == "kt":
                        i = int(name[2:])
                        if i == 0:
                            pe.wait_ge(qs, j * 2 + 2)
                        for a in (range(8) if i == 0 else range(8, 3 * NT)):
                            c, h = divmod(a, 3)
                            m = nc.tensor.transpose(s[0:tok(c), (a % 8) * P:(a % 8 + 1) * P], K[:, h, c * P:c * P + tok(c)], ident[:, :])
                    elif name[:2] == "ds":
                        i = int(name[2:])
                        pe.wait_ge(k_tok, j + 1)
                        for c in (2 * i, 2 * i + 1):
                            for h, (a, b) in enumerate(((0, 256), (256, 384), (384, 512))):
                                o = (c % 2) * 512
                                m = nc.tensor.matmul(s[:, o + a:o + b], k_t[:, c, h * P:(h + 1) * P], v_t[:, c, a:b], start=True, stop=True)
                    elif name[0] == "o":
                        d = int(name[1:])
                        h = head_of[d]
                        cols = slice(d * P, (d + 1) * P)
                        if d == 0:
                            pe.wait_ge(a_s, j + 1)
                            pe.wait_ge(sp_s, j * 2 + 2)
                            pe.wait_ge(st_in, j * 48 + 48)
                        for c in range(NC):
                            m = nc.tensor.matmul(s[:, c * C:(c + 1) * C], v_t[:, c, cols], Am[:, 3 * c + h, :], start=True, stop=(c == 0))
                            if c > 0:
                                m = nc.tensor.matmul(s[:, c * C:(c + 1) * C], sp_t[:, c - 1, cols], Q[:, h, c * C:(c + 1) * C],
                                                     start=False, stop=True)
                        for b in range(NB):
                            st = ssg[:, b, cols] if d < 2 else ssh[:, b, d - 2, :]
                            nc.tensor.matmul(s[:, TP + b * SL:TP + (b + 1) * SL], st, Q[:, h, TP + b * SL:TP + (b + 1) * SL],
                                             start=(b == 0), stop=False, skip_group_check=True)
                        m = nc.tensor.matmul(s[:, TP:T], v_t[0:TS, NC, cols], As[:, h, :], start=False, stop=True, skip_group_check=True)
                    elif name[:4] == "norm":
                        h = int(name[4:])
                        pe.wait_ge(o_sq, j * 4 + (2, 3, 4)[h])
                        for a, b in ((0, TP), (TP, T)):
                            for d in ((0, 1), (2,), (3,))[h]:
                                m = nc.tensor.matmul(s[:, a:b], ones[:, :], sqo[d][:, a:b], start=(d in (0, 2, 3)), stop=(d in (1, 2, 3)))
                    elif name[:2] == "ss":
                        i = int(name[2:])
                        pe.wait_ge(kblk_s, j * 3 + (1, 1, 2, 3)[i])
                        for b in (range(4 * i, 4 * i + 4) if i < 2 else range(NB)):
                            if i < 2:
                                o, v = (b % 4) * DVG, v_t[0:TS, NC, 0:DVG]
                            else:
                                o, v = b * P, v_t[0:TS, NC, i * P:(i + 1) * P]
                            m = nc.tensor.matmul(s[:, o:o + v.shape[-1]], kblk[:, b, :], v, start=True, stop=True)
                    m.then_inc(step_done, 1)

                for n in range(NU):
                    pe.wait_ge(unit_free, j18 + (n + 1))
                    pe.wait_ge(w_lo, j18 + (n + 3))
                    unit_passes(n + 1, proj(n + 1), xh, xl).then_inc(unit_done, 1)
                    for name in AFTER.get(n, []):
                        do_step(name)
    sa.close()

    so = ExitStack()
    sbk = ExitStack()
    g_post = sb("g_post", [P, D], F32, sbk)
    mt = sb("mt", [P, KT, T], F32, sbk)
    hn = sb("hn", [P, 2, D], F32, sbk)
    msq = sb("msq", [P, D], F32, sbk)
    h_in = sem("h_in")
    m_hi = sem("m_hi")
    m_lo = sem("m_lo")
    mt_s = sem("mt_s")
    m_tok = sem("m_tok")
    m_rms = sem("m_rms")
    m_half = sem("m_half")
    h_s = sem("h_s")
    h_rms = sem("h_rms")
    hn_s = sem("hn_s")
    h_turn = sem("h_turn")
    f_hi = sem("f_hi")
    f_lo = sem("f_lo")
    with nc.Block() as block:
        @block.sync
        def _(sp):
            sp.wait_ge(st_out, 80 * G)
            for c in range(NT):
                sp.dma_start(h_t[0:tok(c), c, :], xp_v[c] if c < NC else xs_v).then_inc(h_in, 16)
            sp.dma_start(g_post[:, :], norm_mix_post.partition_broadcast(P).rearrange("p o d -> p (o d)")).then_inc(h_in, 16)
            for u in range(UB + 2, UC + 2):
                sp.wait_ge(w_lo, u)
                src = wout_v[:, :, (u - UB) * P:(u - UB + 1) * P] if u < UC else wf1_v[:, :, (u - UC) * FF:(u - UC) * FF + P]
                load_unit(sp, u, src)

        @block.scalar
        def _(act):
            for k in range(KT):
                act.activation(x_hi[:, k, :], merged[:, k, :], ACT.Copy).then_inc(m_hi, 1)
            for u in range(UB, UC):
                act.wait_ge(w_raw[(u + 2) % NRAW], loaded(u + 2))
                act.wait_ge(unit_done, u)
                split_hi(u + 2)
                act.wait_ge(unit_done, u + 1)
                act.activation(halves(mt[:, u - UB, :]), proj(u), ACT.Copy).then_inc(unit_free, 1)
            for c in range(NT):
                n = tok(c)
                act.wait_ge(m_tok, c + 1)
                act.drain()
                act.activation(msq[0:n, :], tok_slot(ps, c)[0:n, :], ACT.Square, accum_out=stat[0:n, 0, c:c + 1])
                act.drain()
                act.activation(stat[0:n, 1, c:c + 1], stat[0:n, 0, c:c + 1], ACT.Ln, scale=1.0 / D, bias=eps_c[0:n, :])
                act.drain()
                act.activation(stat[0:n, 1, c:c + 1], stat[0:n, 1, c:c + 1], ACT.Exp, scale=-0.5).then_inc(m_rms, 1)
                act.wait_ge(h_s, c + 1)
                act.activation(msq[0:n, :], h_t[0:n, c, :], ACT.Square, accum_out=stat[0:n, 0, c:c + 1])
                act.drain()
                act.activation(stat[0:n, 1, c:c + 1], stat[0:n, 0, c:c + 1], ACT.Ln, scale=1.0 / D, bias=eps_c[0:n, :])
                act.drain()
                act.activation(stat[0:n, 1, c:c + 1], stat[0:n, 1, c:c + 1], ACT.Exp, scale=-0.5).then_inc(h_rms, 1)
                act.wait_ge(h_turn, c + 1)
                for q in range(2):
                    s = tok_slot(ps, c)[:, q * 512:(q + 1) * 512].rearrange("p (k t) -> p k t", k=4)
                    for k in range(4):
                        ins = act.activation(x_hi[:, 4 * q + k, c * P:c * P + n], s[:, k, 0:n], ACT.Copy,
                                             scale=gain[:, 1, 4 * q + k:4 * q + k + 1])
                ins.then_inc(f_hi, 1)

        @block.vector
        def _(dve):
            for k in range(KT):
                dve.wait_ge(m_hi, k + 1)
                dve.tensor_tensor(x_lo[:, k, :], merged[:, k, :], x_hi[:, k, :].bitcast(F32), ALU.subtract).then_inc(m_lo, 1)
            for u in range(UB, UC):
                dve.wait_ge(w_hi, u + 3)
                split_lo(u + 2)
            dve.wait_ge(h_in, 16 * (NT + 1))
            for c in range(NT):
                n = tok(c)
                dve.wait_ge(m_rms, c + 1)
                if c >= 2:
                    dve.wait_ge(h_turn, c - 1)
                dve.scalar_tensor_tensor(hn[0:n, c % 2, :], tok_slot(ps, c)[0:n, :], stat[0:n, 1, c:c + 1], g_post[0:n, :],
                                         ALU.mult, ALU.mult).then_inc(m_half, 1)
                dve.drain()
                dve.tensor_tensor(h_t[0:n, c, :], h_t[0:n, c, :], hn[0:n, c % 2, :], ALU.add).then_inc(h_s, 1)
                dve.wait_ge(h_rms, c + 1)
                dve.tensor_scalar(hn[0:n, c % 2, :], h_t[0:n, c, :], stat[0:n, 1, c:c + 1], None, ALU.mult).then_inc(hn_s, 1)
                dve.wait_ge(f_hi, c + 1)
                for q in range(2):
                    s = tok_slot(ps, c)[:, q * 512:(q + 1) * 512].rearrange("p (k t) -> p k t", k=4)
                    for k in range(4):
                        ins = dve.scalar_tensor_tensor(x_lo[:, 4 * q + k, c * P:c * P + n], s[:, k, 0:n],
                                                       gain[:, 1, 4 * q + k:4 * q + k + 1],
                                                       x_hi[:, 4 * q + k, c * P:c * P + n].bitcast(F32), ALU.mult, ALU.subtract)
                ins.then_inc(f_lo, 1)

        @block.tensor
        def _(pe):
            for u in range(UB, UC):
                pe.wait_ge(unit_free, u)
                pe.wait_ge(w_lo, u + 2)
                if u == UB:
                    pe.wait_ge(m_lo, KT)
                unit_passes(u, proj(u), xh, xl).then_inc(unit_done, 1)

            def turn_m(c):
                if c >= 4:
                    pe.wait_ge(f_lo, c - 3)
                for k in range(KT):
                    m = nc.tensor.transpose(tok_slot(ps, c)[0:tok(c), k * P:(k + 1) * P], mt[:, k, c * P:c * P + tok(c)], ident[:, :])
                m.then_inc(m_tok, 1)

            pe.wait_ge(unit_free, UC + 1)
            for c in range(4):
                turn_m(c)
            for c in range(NT):
                n = tok(c)
                if c == 4:
                    turn_m(4)
                pe.wait_ge(m_half, c + 1)
                pe.wait_ge(hn_s, c + 1)
                for k in range(KT):
                    m = nc.tensor.transpose(tok_slot(ps, c)[:, k * P:k * P + n], hn[0:n, c % 2, k * P:(k + 1) * P], ident[0:n, 0:n])
                m.then_inc(h_turn, 1)
    sbk.close()
    merged_stack.close()

    act_hi = sb("act_hi", [P, FT, T], F32R)
    act_lo = sb("act_lo", [P, FT, T], F32R)
    sc = ExitStack()
    fe = sb("fe", [P, 2, T], F32, sc)
    fa = sb("fa", [P, 2, T], F32, sc)
    hs_out = sem("hs_out")
    ff_a = sem("ff_a")
    ff_d = sem("ff_d")
    ff_h = sem("ff_h")
    ff_l = sem("ff_l")
    PAIRS = 3
    LOOPS = (FT - 1) // PAIRS
    with nc.Block() as block:
        @block.sync
        def _(sp):
            sp.dma_start(ys_v, h_t[0:TS, NC, :]).then_inc(hs_out, 16)
            with nc.sync.Fori(0, LOOPS) as i:
                i6 = sp.snap(i * 2 * PAIRS)
                for n in range(2 * PAIRS):
                    first = sp.snap(i * (PAIRS * P) + ((n // 2 + 1) * P + n % 2 * FF))
                    sp.wait_ge(w_lo, i6 + (UC + 2 + n))
                    load_unit(sp, UC + 2 + n, wf1_v[:, :, bass.ds(first, P)])
            for n in range(2):
                sp.wait_ge(w_lo, UD + n)
                load_unit(sp, UD + n, wf2_v[:, KCUT[n][0]:KCUT[n][0] + KCUT[n][1], 0:P], KCUT[n][1])

        @block.scalar
        def _(act):
            scratch = act.alloc_register("act_scratch_c")
            act.reg_mov(scratch, 0)

            def pair(i6, i3, p):
                for n in (2 * p, 2 * p + 1):
                    held(act, scratch, w_raw[(UC + n + 2) % NRAW], loaded(UC + n + 2, i3))
                    held(act, scratch, unit_done, i6 + (UC + n))
                    split_hi(UC + n + 2, KT)
                    held(act, scratch, unit_done, i6 + (UC + n + 1))
                    if n % 2 == 0:
                        held(act, scratch, ff_l, i3 + (p + 1))
                        act.activation(halves(fe[:, 0, :]), proj(UC + n), ACT.Exp, scale=-1.0)
                        act.activation(halves(fa[:, 0, :]), proj(UC + n), ACT.Copy).then_inc(unit_free, 1)
                        act.drain().then_inc(ff_a, 1)
            with nc.scalar.Fori(0, LOOPS) as i:
                i6 = act.snap(i * 2 * PAIRS)
                i3 = act.snap(i * PAIRS)
                for p in range(PAIRS):
                    pair(i6, i3, p)
            pair(2 * PAIRS * LOOPS, PAIRS * LOOPS, 0)

        @block.vector
        def _(dve):
            dve.memset(fe[:, :, 0:1], 0.0).then_inc(ff_l, 1)

            def pair(i6, i3, p, row):
                for n in (2 * p, 2 * p + 1):
                    dve.wait_ge(w_hi, i6 + (UC + n + 3))
                    split_lo(UC + n + 2)
                dve.wait_ge(ff_a, i3 + (p + 1))
                dve.tensor_scalar(fe[:, 0, :], fe[:, 0, :], 1.0, None, ALU.add)
                dve.drain()
                dve.reciprocal(fe[:, 0, :], fe[:, 0, :])
                dve.drain()
                dve.tensor_tensor(fa[:, 0, :], fa[:, 0, :], fe[:, 0, :], ALU.mult)
                dve.drain()
                dve.wait_ge(unit_done, i6 + (UC + 2 * p + 2))
                dve.tensor_tensor(halves(fe[:, 0, :]), halves(fa[:, 0, :]), proj(UC + 2 * p + 1), ALU.mult).then_inc(unit_free, 1)
                dve.drain()
                dve.tensor_copy(act_hi[:, row, :], fe[:, 0:1, :])
                dve.drain()
                dve.tensor_tensor(act_lo[:, row, :], fe[:, 0:1, :], act_hi[:, row, :].bitcast(F32), ALU.subtract).then_inc(ff_l, 1)
            with nc.vector.Fori(0, LOOPS) as i:
                i6 = dve.snap(i * 2 * PAIRS)
                i3 = dve.snap(i * PAIRS)
                for p in range(PAIRS):
                    pair(i6, i3, p, bass.ds(i * PAIRS + p, 1))
            pair(2 * PAIRS * LOOPS, PAIRS * LOOPS, 0, slice(FT - 1, FT))

        @block.tensor
        def _(pe):
            def pair(i6, p):
                for n in (2 * p, 2 * p + 1):
                    pe.wait_ge(unit_free, i6 + (UC + n))
                    pe.wait_ge(w_lo, i6 + (UC + n + 2))
                    unit_passes(UC + n, proj(UC + n), xh, xl).then_inc(unit_done, 1)
            with nc.tensor.Fori(0, LOOPS) as i:
                i6 = pe.snap(i * 2 * PAIRS)
                for p in range(PAIRS):
                    pair(i6, p)
            pair(2 * PAIRS * LOOPS, 0)
    sc.close()

    f_t = sb("f_t", [P, T])
    f_main = sb("f_main", [P, NC, D])
    f_tok = [f_main[:, c, :] for c in range(NC)] + [h_t[:, NC, :]]
    h_back = w_raw_t[:, 1, :, :].rearrange("p k n -> p (k n)")
    h_tok = [h_t[:, c, :] for c in range(NC)] + [h_back]
    g_last = w_raw_t[:, 0, :, :].rearrange("p k n -> p (k n)")
    g_in = sem("g_in")
    ft_s = sem("ft_s")
    ft_turn = sem("ft_turn")
    ft_tok = sem("ft_tok")
    y_rms = sem("y_rms")
    y_s = sem("y_s")
    y_out = sem("y_out")
    TILES = 2
    NCUT = len(KCUT)
    BODY = TILES * NCUT
    LOOPD = KT // TILES
    with nc.Block() as block:
        def g_sq(c, n):
            return ps[0:n, 0:2, :].rearrange("p a b -> p (a b)")

        @block.sync
        def _(sp):
            def loads(i6, col, ns):
                for n in ns:
                    k0, nk = KCUT[n % NCUT]
                    where = col(n // NCUT)
                    sp.wait_ge(w_lo, i6 + (UD + n))
                    load_unit(sp, UD + n, wf2_v[:, k0:k0 + nk, where], nk)
            with nc.sync.Fori(0, LOOPD - 1) as i:
                i6 = sp.snap(i * BODY)
                loads(i6, lambda t: bass.ds(sp.snap(i * (TILES * P) + t * P), P), range(2, BODY + 2))
            i6 = (LOOPD - 1) * BODY
            loads(i6, lambda t: slice((LOOPD - 1) * TILES * P + t * P, (LOOPD - 1) * TILES * P + (t + 1) * P), range(2, BODY))
            sp.wait_ge(hs_out, 16)
            sp.wait_ge(w_lo, UD + KT * NCUT + 1)
            sp.dma_start(g_last, norm_ffn_post.partition_broadcast(P).rearrange("p o d -> p (o d)")).then_inc(g_in, 16)
            sp.dma_start(h_back[0:TS, :], ys_v).then_inc(g_in, 16)
            sp.wait_ge(g_in, 32)
            for c in range(NT):
                sp.wait_ge(y_s, c + 1)
                sp.dma_start(yp_v[c] if c < NC else ys_v, f_tok[c][0:tok(c), :]).then_inc(y_out, 16)
            sp.wait_ge(y_out, 16 * NT)

        @block.gpsimd
        def _(pool):
            pool.wait_ge(st_out, 80 * G)

        @block.scalar
        def _(act):
            scratch = act.alloc_register("act_scratch_d")
            act.reg_mov(scratch, 0)

            def body(i6, i3, i2, last):
                for n in range(BODY):
                    if not last or n < BODY - 2:
                        held(act, scratch, w_raw[(UD + n + 2) % NRAW], loaded(UD + n + 2, i3))
                        held(act, scratch, unit_done, i6 + (UD + n))
                        split_hi(UD + n + 2, KCUT[(n + 2) % NCUT][1])
                    if n % NCUT == NCUT - 1:
                        m = n // NCUT
                        held(act, scratch, unit_done, i6 + (UD + n + 1))
                        held(act, scratch, ft_tok, i2 + (m + 2))
                        act.activation(halves(f_t[:, :]), proj(m), ACT.Copy).then_inc(ft_s, 1)
            with nc.scalar.Fori(0, LOOPD - 1) as i:
                body(act.snap(i * BODY), act.snap(i * (BODY // NRAW)), act.snap(i * TILES), False)
            body((LOOPD - 1) * BODY, (LOOPD - 1) * BODY // NRAW, (LOOPD - 1) * TILES, True)
            act.wait_ge(ft_tok, KT + 2)
            for c in range(NT):
                n = tok(c)
                act.activation(g_sq(c, n), f_tok[c][0:n, :], ACT.Square, accum_out=stat[0:n, 0, c:c + 1])
                act.drain()
                act.activation(stat[0:n, 1, c:c + 1], stat[0:n, 0, c:c + 1], ACT.Ln, scale=1.0 / D, bias=eps_c[0:n, :])
                act.drain()
                act.activation(stat[0:n, 1, c:c + 1], stat[0:n, 1, c:c + 1], ACT.Exp, scale=-0.5).then_inc(y_rms, 1)

        @block.vector
        def _(dve):
            for _ in range(2):
                dve.drain().then_inc(ft_tok, 1)

            def body(i6, i2, last, tile):
                for n in range(BODY):
                    if not last or n < BODY - 2:
                        dve.wait_ge(w_hi, i6 + (UD + n + 3))
                        split_lo(UD + n + 2, KCUT[(n + 2) % NCUT][1])
                    if n == NCUT + 1:
                        take(i2, 0, tile)
                take(i2, 1, tile)

            dve.wait_ge(hs_out, 16)

            def take(i2, m, tile):
                dve.wait_ge(ft_turn, i2 + (m + 1))
                s = slot(m)
                dve.tensor_copy(f_main[:, :, tile(m)], s[:, 0:TP].rearrange("p (c v) -> p c v", c=NC))
                dve.tensor_copy(f_tok[NC][0:TS, tile(m)], s[0:TS, TP:TP + P]).then_inc(ft_tok, 1)
            with nc.vector.Fori(0, LOOPD - 1) as i:
                body(dve.snap(i * BODY), dve.snap(i * TILES), False, lambda m: bass.ds(i * (TILES * P) + m * P, P))
            base = (LOOPD - 1) * TILES * P
            body((LOOPD - 1) * BODY, (LOOPD - 1) * TILES, True, lambda m: slice(base + m * P, base + (m + 1) * P))
            dve.wait_ge(g_in, 32)
            dve.drain()
            for c in range(NT):
                n = tok(c)
                dve.wait_ge(y_rms, c + 1)
                dve.scalar_tensor_tensor(f_tok[c][0:n, :], f_tok[c][0:n, :], stat[0:n, 1, c:c + 1], g_last[0:n, :], ALU.mult, ALU.mult)
                dve.drain()
                dve.tensor_tensor(f_tok[c][0:n, :], f_tok[c][0:n, :], h_tok[c][0:n, :], ALU.add).then_inc(y_s, 1)

        @block.tensor
        def _(pe):
            def turn(i2, m):
                pe.wait_ge(ft_s, i2 + (m + 1))
                for c in range(NT):
                    ins = nc.tensor.transpose(slot(m)[0:tok(c), c * P:(c + 1) * P], f_t[:, c * P:c * P + tok(c)], ident[:, :])
                ins.then_inc(ft_turn, 1)

            def body(i6, i2):
                for n in range(BODY):
                    m, cut = divmod(n, NCUT)
                    k0, nk = KCUT[cut]
                    pe.wait_ge(w_lo, i6 + (UD + n + 2))
                    if cut == 0:
                        pe.wait_ge(ft_tok, i2 + (m + 1))
                    unit_passes(UD + n, proj(m), lambda k, q: act_hi[:, k0 + k, q * HT:(q + 1) * HT],
                                lambda k, q: act_lo[:, k0 + k, q * HT:(q + 1) * HT], nk,
                                first=(cut == 0), last=(cut == NCUT - 1)).then_inc(unit_done, 1)
                    if m == 1 and cut == 0:
                        turn(i2, 0)
                turn(i2, 1)
            with nc.tensor.Fori(0, LOOPD - 1) as i:
                body(pe.snap(i * BODY), pe.snap(i * TILES))
            body((LOOPD - 1) * BODY, (LOOPD - 1) * TILES)
    keep.close()


LOG2_40 = 27.725887222397812
CONSTS = 6 + 3 + 2 * NL + 2
SETUP = 1
LEVEL_AT = {6: 0, 8: 1, 10: 2, 11: 3, 13: 4, 14: 5, 15: 6}


def turn_slot(ps, k):
    return ps[:, 2 * (k % 4):2 * (k % 4) + 2, :].rearrange("p a b -> p (a b)")


def tok_slot(ps, c):
    return ps[:, 2 * (c % 4):2 * (c % 4) + 2, :].rearrange("p a b -> p (a b)")


_INS = ["x_prompt", "x_sample", "state_gla", "state_hgrn", "norm_mix_pre", "norm_mix_post", "norm_ffn_pre",
        "norm_ffn_post", "w_in", "gla_w_lr2", "gla_b_lr", "gla_onorm", "hgrn_lb", "hgrn_onorm", "w_out",
        "w_ffn_in", "w_ffn_out"]
_BY_FEATURE = ("norm_mix_pre", "norm_ffn_pre", "gla_b_lr", "gla_onorm", "hgrn_lb", "hgrn_onorm")
_OUTS = [((1, 512, 1024), "float32"), ((8, 8, 1024), "float32"), ((1, 1, 4, 128, 256), "float32"),
         ((1, 8, 4, 128, 256), "float32"), ((1, 1, 8, 128, 128), "float32"), ((1, 8, 8, 128, 128), "float32")]


def kernel(**inputs):
    import numpy as _np
    import concourse.bacc as _bacc
    from concourse import mybir as _mybir
    from concourse.bass_utils import run_bass_kernel_spmd as _run

    nc = _bacc.Bacc("TRN2", target_bir_lowering=False, num_devices=1)
    arrays, args = {}, []
    for name in _INS:
        a = inputs[name]
        if name in _BY_FEATURE:
            a = _np.asarray(a).reshape(-1, 128).T
        a = _np.ascontiguousarray(a)
        arrays[f"in_{name}_dram"] = a
        args.append(nc.dram_tensor(f"in_{name}_dram", a.shape, _mybir.dt.from_np(a.dtype), kind="ExternalInput").ap())
    for i, (shape, dtype) in enumerate(_OUTS):
        dt = _mybir.dt.from_np(_np.dtype(dtype))
        args.append(nc.dram_tensor(f"out_{i}_dram", shape, dt, kind="ExternalOutput").ap())
    build(nc, *args)
    r = _run(nc, [arrays], core_ids=[0])
    return tuple(r.results[0][f"out_{i}_dram"] for i in range(len(_OUTS)))
```

```python
from contextlib import ExitStack

import concourse.bass as bass
import concourse.mybir as mybir

ALU = mybir.AluOpType
ACT = mybir.ActivationFunctionType
F32 = mybir.dt.float32
F32R = mybir.dt.float32r
I32 = mybir.dt.int32

P = 128
D = 1024
KT = D // P
TP, NB, SL = 512, 8, 8
TS = NB * SL
T = TP + TS
HT = T // 2
C = 128
NC = TP // C
NT = NC + 1
GH, HH = 4, 8
GR, DVG = 16, 256
FF = 2816
FT = FF // P
EPS = 1e-6
TAU = 16.0
LEVELS = (1, 2, 4, 8, 16, 32, 64)
NL = len(LEVELS)
G = GH
ENDS = [0]
for _w in (512, 512, 1024, 1024, GR, 1024, 1024, 1024, 1024, 1024, 1024):
    ENDS.append(ENDS[-1] + _w)
GQ, GK, GV, GG, GLR, HQ, HF, HI, HG, GA, GB = ENDS[:-1]

UNITS = [(HF, 256, 0), (HF, 256, 1), (GK, 128, 0), (GQ, 128, 0), (HQ, 256, 0), (HQ, 256, 1),
         (GV, 256, 0), (GV, 256, 1), (HI, 256, 0), (HI, 256, 1),
         (GA, 256, 0), (GG, 256, 0), (GA, 256, 1), (GG, 256, 1),
         (GB, 256, 0), (HG, 256, 0), (GB, 256, 1), (HG, 256, 1)]
NU = len(UNITS)
GATE0 = 10
UB = 1 + G * NU
UC = UB + D // P
UD = UC + 2 * FT
KCUT = ((0, 8), (8, 8), (16, 6))
NRAW, NSPL = 2, 3

AFTER = {1: ["decay"], 6: ["diag0", "diag1", "diag2"], 7: ["level0", "v0"], 8: ["level1", "v1"], 9: ["level2", "v2"],
         10: ["level3", "v3"], 11: ["level4"], 12: ["level5"], 13: ["level6"], 14: ["kt0", "kt1"], 15: ["ds0", "ds1"],
         16: ["o0", "o1", "o2"], 17: ["o3", "ss0", "ss1", "ss2", "ss3", "norm0", "norm1", "norm2"]}
STEPS = [s for n in range(NU) for s in AFTER.get(n, [])]
NR = len(STEPS)
STEP = {name: r for r, name in enumerate(STEPS)}
assert NR % 2 == 0


def build(nc, x_prompt, x_sample, state_gla, state_hgrn, norm_mix_pre, norm_mix_post, norm_ffn_pre,
          norm_ffn_post, w_in, gla_w_lr2, gla_b_lr, gla_onorm, hgrn_lb, hgrn_onorm, w_out, w_ffn_in,
          w_ffn_out, y_prompt, y_sample, gla_prompt, gla_sample, hgrn_prompt, hgrn_sample):
    keep = ExitStack()

    def sb(name, shape, dt=F32, on=None):
        return (on or keep).enter_context(nc.sbuf_tensor(name, shape, dt))

    def sem(name):
        return keep.enter_context(nc.semaphore(name))

    x_hi = sb("x_hi", [P, KT, T], F32R)
    x_lo = sb("x_lo", [P, KT, T], F32R)
    w_raw_t = sb("w_raw_t", [P, NRAW, KT, P])
    w_hi_t = sb("w_hi_t", [P, NSPL, KT, P], F32R)
    w_lo_t = sb("w_lo_t", [P, NSPL, KT, P], F32R)
    ident = sb("ident", [P, P])
    eps_c = sb("eps_c", [P, 1])
    one_c = sb("one_c", [P, 1])
    gain = sb("gain", [P, 3, KT])
    stat = sb("stat", [P, 2, NT])
    h_t = sb("h_t", [P, NT, D])
    ps = keep.enter_context(nc.psum_tensor("ps", [P, 8, 512], F32))

    def proj(u):
        return ps[:, 2 * (u % 2):2 * (u % 2) + 2, 0:HT]

    def slot(r):
        return ps[:, 4 + 2 * (r % 2):6 + 2 * (r % 2), :].rearrange("p a b -> p (a b)")

    def halves(ap):
        return ap.rearrange("p (a b) -> p a b", a=2)

    w_raw = [sem(f"w_raw{i}") for i in range(NRAW)]
    w_hi = sem("w_hi")
    w_lo = sem("w_lo")
    unit_done = sem("unit_done")
    unit_free = sem("unit_free")
    step_done = sem("step_done")
    step_free = [sem("step_free0"), sem("step_free1")]
    small = sem("small")
    consts = sem("consts")
    setup = sem("setup")
    x_in = sem("x_in")
    squared = sem("squared")
    scaled = sem("scaled")
    turned = sem("turned")
    x_hi_s = sem("x_hi_s")
    x_lo_s = sem("x_lo_s")
    lb_a = sem("lb_a")
    lb_d = sem("lb_d")
    grp_in = sem("grp_in")
    st_in = sem("st_in")
    st_out = sem("st_out")
    lbj_s = sem("lbj_s")
    z_abs = sem("z_abs")
    l_dve = sem("l_dve")
    l2_act = sem("l2_act")
    qk_in = sem("qk_in")
    lvl = sem("lvl")
    qs = sem("qs")
    dec_s = sem("dec_s")
    a_s = sem("a_s")
    v_in = sem("v_in")
    v_tok = sem("v_tok")
    k_tok = sem("k_tok")
    sp_s = sem("sp_s")
    kblk_s = sem("kblk_s")
    ss_s = sem("ss_s")
    gate_in = sem("gate_in")
    gate_s = sem("gate_s")
    o_sq = sem("o_sq")
    rst = sem("rst")
    merged_s = sem("merged_s")
    glr_s = sem("glr_s")

    v2 = lambda w: w.rearrange("o (k p) n -> p (o k) n", p=P)
    win_v, wout_v, wf1_v, wf2_v = v2(w_in), v2(w_out), v2(w_ffn_in), v2(w_ffn_out)
    xp_v = x_prompt.rearrange("o (c p) d -> c p (o d)", p=P)
    xs_v = x_sample.rearrange("b t d -> (b t) d")
    yp_v = y_prompt.rearrange("o (c p) d -> c p (o d)", p=P)
    ys_v = y_sample.rearrange("b t d -> (b t) d")
    tok = lambda c: P if c < NC else TS

    def held(eng, scratch, s, value):
        eng.wait_ge(s, value)
        eng.reg_alu(scratch, scratch, 1, ALU.add)

    def load_unit(eng, u, src, nk=KT):
        eng.dma_start(w_raw_t[:, u % NRAW, 0:nk, :], src).then_inc(w_raw[u % NRAW], 16)

    def loaded(u, more=0):
        return more * 16 + 16 * (u // NRAW + 1)

    def split_hi(u, nk=KT):
        nc.scalar.activation(w_hi_t[:, u % NSPL, 0:nk, :], w_raw_t[:, u % NRAW, 0:nk, :],
                             ACT.Copy).then_inc(w_hi, 1)

    def split_lo(u, nk=KT):
        nc.vector.tensor_tensor(w_lo_t[:, u % NSPL, 0:nk, :], w_raw_t[:, u % NRAW, 0:nk, :],
                                w_hi_t[:, u % NSPL, 0:nk, :].bitcast(F32), ALU.subtract).then_inc(w_lo, 1)

    def unit_passes(u, out, hi, lo, nk=KT, first=True, last=True):
        todo = [(w, x, k) for k in range(nk) for w, x in ((w_lo_t, hi), (w_hi_t, lo), (w_hi_t, hi))]
        for i, (w, x, k) in enumerate(todo):
            for q in range(2):
                m = nc.tensor.matmul(out[:, q, :], w[:, u % NSPL, k, :], x(k, q),
                                     start=first and i == 0, stop=last and i == len(todo) - 1)
        return m

    xh = lambda k, q: x_hi[:, k, q * HT:(q + 1) * HT]
    xl = lambda k, q: x_lo[:, k, q * HT:(q + 1) * HT]

    merged_stack = ExitStack()
    merged = sb("merged", [P, KT, T], F32, merged_stack)
    sa = ExitStack()
    A = lambda name, shape, dt=F32: sb(name, shape, dt, sa)
    Z = A("Z", [P, 3, T])
    L4 = A("L4", [P, 4, T])
    T3 = A("T3", [P, 3, T])
    B = A("B", [P, 3, T])
    Q = A("Q", [P, 3, T])
    K = A("K", [P, 3, T])
    Am = A("Am", [P, NC * 3, C])
    As = A("As", [TS, 3, TS])
    v_t = A("v_t", [P, NT, 4 * P])
    k_t = A("k_t", [P, NT, 3 * P])
    sp_t = A("sp_t", [P, NC, 4 * P])
    ssg = h_t[:, 0:2, :].rearrange("p a (b v) -> p (a b) v", v=DVG)
    ssh = h_t[:, 2:4, :].rearrange("p a (b h v) -> p (a b) h v", h=2, v=P)
    Gt = A("Gt", [P, 4, T])
    E2 = A("E2", [P, 2, T])
    glr = A("glr", [GR, T])
    wlr = A("wlr", [GR, P])
    blr4 = A("blr4", [P, GH])
    blr = A("blr", [P, 1])
    ones = A("ones", [P, P])
    mask = A("mask", [P, NL, C // 2])
    rowm = A("rowm", [TS, NB])
    tick = A("tick", [1, 1])
    pool_w = A("pool_w", [1, 2])
    onm = A("onm", [P, 3])
    lb = A("lb", [P, 6, HH])
    lbj = A("lbj", [P, 2, 2])
    dec = A("dec", [P, 3, NC + NB])
    k_flat = k_t[:, :, :].rearrange("p a b -> p (a b)")
    kblk = [t[:, :, :].rearrange("p a b -> p (a b)")[0:TS, 0:NB * P].rearrange("p (b d) -> p b d", b=NB)
            for t in (T3, B, T3)]
    over, at = {1: Z[:, :, :]}, 0
    for L in (2, 4, 8, 16, 32, 64, 128):
        blocks = (T if L <= SL else TP) // L
        over[L] = B[:, :, :].rearrange("p a b -> p (a b)")[:, at:at + 3 * blocks].rearrange("p (h n) -> p h n", h=3)
        at += 3 * blocks
    assert at <= 3 * T
    xt = [h_t[:, c, :] for c in range(NT)]
    square = v_t[:, :, :].rearrange("p a b -> p (a b)")[:, 0:D]
    sqo = [Z[:, 0, :], Z[:, 1, :], Z[:, 2, :], T3[:, 2, :]]
    head_of = (0, 0, 1, 2)

    def second(ap, L):
        return ap.rearrange("p (n b) -> p n b", b=2 * L)[:, :, L:2 * L]

    block = nc.Block()
    with block:
        @block.sync
        def _(sp):
            for c in range(NT):
                sp.dma_start(xt[c][0:tok(c), :], xp_v[c] if c < NC else xs_v).then_inc(x_in, 16)
            for t, v in ((gain[:, 0, :], norm_mix_pre), (gain[:, 1, :], norm_ffn_pre), (gain[:, 2, :], hgrn_lb),
                         (onm[:, 0:2], gla_onorm), (onm[:, 2:3], hgrn_onorm), (blr4[:, :], gla_b_lr)):
                sp.dma_start(t, v).then_inc(small, 16)
            load_unit(sp, 0, win_v[:, :, GLR:GLR + P])
            with nc.sync.Fori(0, G) as j:
                j18 = sp.snap(j * NU)
                for n, (col, width, t) in enumerate(UNITS):
                    first = (j * (width // P) + (col // P + t)) * P + col % P
                    sp.wait_ge(w_lo, j18 + (n + 1))
                    load_unit(sp, n + 1, win_v[:, :, bass.ds(first, P)])
            for u in range(UB, UB + 2):
                sp.wait_ge(w_lo, u)
                load_unit(sp, u, wout_v[:, :, (u - UB) * P:(u - UB + 1) * P])
            sp.wait_ge(w_lo, UB + 2)

        @block.gpsimd
        def _(pool):
            n = 0

            def hold(s, value):
                pool.wait_ge(s, value)
                nc.gpsimd.tensor_tensor(pool_w[:, 1:2], pool_w[:, 0:1], pool_w[:, 0:1], ALU.add)
                pool.drain()
            for t in (ident, ones, mask, rowm, pool_w):
                ins = nc.gpsimd.memset(t[:], 0.0 if t is ident else 1.0)
                ins.then_inc(consts, 1)
                n += 1
            pool.wait_ge(consts, n)
            nc.gpsimd.affine_select(out=ident[:], in_=ident[:], compare_op=ALU.not_equal, fill=1.0, base=0,
                                    pattern=[[-1, P]], channel_multiplier=1).then_inc(consts, 1)
            n += 1
            for i, L in enumerate(LEVELS):
                m = mask[:, i, :].rearrange("p (a r) -> p a r", r=L)
                nc.gpsimd.affine_select(out=m, in_=m, compare_op=ALU.is_ge, fill=0.0, base=0,
                                        pattern=[[-2 * L, C // 2 // L], [0, L]], channel_multiplier=1).then_inc(consts, 1)
                n += 1
                pool.wait_ge(consts, n)
                nc.gpsimd.affine_select(out=m, in_=m, compare_op=ALU.is_ge, fill=0.0, base=L - 1,
                                        pattern=[[2 * L, C // 2 // L], [0, L]], channel_multiplier=-1).then_inc(consts, 1)
                n += 1
            nc.gpsimd.affine_select(out=rowm[:], in_=rowm[:], compare_op=ALU.is_ge, fill=0.0, base=0,
                                    pattern=[[-SL, NB]], channel_multiplier=1).then_inc(consts, 1)
            n += 1
            pool.wait_ge(consts, n)
            nc.gpsimd.affine_select(out=rowm[:], in_=rowm[:], compare_op=ALU.is_ge, fill=0.0, base=SL - 1,
                                    pattern=[[SL, NB]], channel_multiplier=-1).then_inc(consts, 1)
            n += 1
            assert n == CONSTS, n
            pool.wait_ge(turned, KT)
            with nc.gpsimd.Fori(0, G) as j:
                pool.dma_start(wlr[:, :], gla_w_lr2[0, :, bass.ds(j * P, P)]).then_inc(grp_in, 16)
                pool.dma_start(ssg[:, :, :], state_gla.rearrange("o b h k v -> k (o b h) v").rearrange(
                    "k (b h) v -> k h b v", h=GH)[:, bass.ds(j, 1), :, :].rearrange("k o b v -> k (o b) v")).then_inc(st_in, 16)
                for i in range(2):
                    pool.dma_start(ssh[:, :, i, :], state_hgrn.rearrange("o b h k v -> k (o b h) v").rearrange(
                        "k (b h) v -> k h b v", h=HH)[:, bass.ds(2 * j + i, 1), :, :].rearrange("k o b v -> k (o b) v")).then_inc(st_in, 16)
                hold(sp_s, j * 2 + 2)
                pool.dma_start(gla_prompt.rearrange("o b h k v -> k (o b h) v")[:, bass.ds(j, 1), :],
                               sp_t[:, NC - 1:NC, 0:DVG]).then_inc(st_out, 16)
                pool.dma_start(hgrn_prompt.rearrange("o b h k v -> k (o b h) v")[:, bass.ds(2 * j, 2), :],
                               sp_t[:, NC - 1, DVG:2 * DVG].rearrange("k (h v) -> k h v", h=2)).then_inc(st_out, 16)
                hold(ss_s, j * 4 + 4)
                pool.dma_start(gla_sample.rearrange("o b h k v -> k (o b h) v").rearrange(
                    "k (b h) v -> k h b v", h=GH)[:, bass.ds(j, 1), :, :].rearrange("k o b v -> k (o b) v"), ssg[:, :, :]).then_inc(st_out, 16)
                for i in range(2):
                    pool.dma_start(hgrn_sample.rearrange("o b h k v -> k (o b h) v").rearrange(
                        "k (b h) v -> k h b v", h=HH)[:, bass.ds(2 * j + i, 1), :, :].rearrange("k o b v -> k (o b) v"), ssh[:, :, i, :]).then_inc(st_out, 16)
                hold(st_out, j * 80 + 80)

        @block.scalar
        def _(act):
            scratch = act.alloc_register("act_scratch")
            act.reg_mov(scratch, 0)
            act.preload_act_table_set("natural_log_exp_and_others")
            act.wait_ge(setup, SETUP)
            for c in range(NT):
                act.wait_ge(x_in, 16 * NT)
                act.activation(square[0:tok(c), :], xt[c][0:tok(c), :], ACT.Square, accum_out=stat[0:tok(c), 0, c:c + 1])
                act.drain()
            act.activation(stat[:, 1, :], stat[:, 0, :], ACT.Ln, scale=1.0 / D, bias=eps_c[:, :])
            act.drain()
            act.activation(stat[:, 1, :], stat[:, 1, :], ACT.Exp, scale=-0.5).then_inc(squared, 1)
            act.wait_ge(lb_d, 1)
            act.activation(lb[:, 1, :], lb[:, 1, :], ACT.Exp).then_inc(lb_a, 1)
            act.wait_ge(lb_d, 2)
            act.activation(lb[:, 5, :], lb[:, 5, :], ACT.Ln, scale=-1.0, bias=one_c[:, :]).then_inc(lb_a, 1)
            for k in range(KT):
                act.wait_ge(turned, k + 1)
                act.activation(x_hi[:, k, :], turn_slot(ps, k)[:, 0:T], ACT.Copy, scale=gain[:, 0, k:k + 1]).then_inc(x_hi_s, 1)
            for u in range(3):
                act.wait_ge(w_raw[u % NRAW], loaded(u))
                split_hi(u)
            act.wait_ge(unit_done, 1)
            act.activation(halves(glr[:, :]), proj(0)[0:GR], ACT.Copy).then_inc(unit_free, 1)
            with nc.scalar.Fori(0, G) as j:
                j18 = act.snap(j * NU)
                jr = act.snap(j * NR)
                hold = lambda s, v: held(act, scratch, s, v)

                def step(name):
                    hold(step_done, jr + (STEP[name] + 1))

                def freed(ins, name):
                    ins.then_inc(step_free[STEP[name] % 2], 1)

                def evacuate(n):
                    hold(unit_done, j18 + (n + 2))
                    src = proj(n + 1)
                    if n < 2:
                        act.activation(halves(Z[:, 1 + n, :]), src, ACT.Copy).then_inc(unit_free, 1)
                    elif n == 2:
                        act.activation(halves(K[:, 0, :]), src, ACT.Copy).then_inc(unit_free, 1)
                    elif n < 6:
                        act.activation(halves(Q[:, n - 3, :]), src, ACT.Copy,
                                       scale=float(P) ** -0.5 if n == 3 else 1.0).then_inc(unit_free, 1)
                    elif n < GATE0:
                        if n == 6:
                            hold(merged_s, j + 1)
                        act.activation(halves(Gt[:, n - 6, :]), src, ACT.Copy).then_inc(unit_free, 1)
                    elif n % 2 == 0:
                        hold(gate_s, j * 4 + ((n - GATE0) // 2 + 1))
                        act.activation(halves(E2[:, 0, :]), src, ACT.Sigmoid).then_inc(unit_free, 1)
                    else:
                        act.activation(halves(E2[:, 1, :]), src, ACT.Sigmoid)
                        act.activation(halves(Gt[:, (n - GATE0) // 2, :]), src, ACT.Copy).then_inc(unit_free, 1)

                def spread(h):
                    for b in range(NB):
                        ins = act.activation(kblk[h][:, b, :], k_t[0:TS, NC, h * P:(h + 1) * P], ACT.Copy, scale=rowm[:, b:b + 1])
                    ins.then_inc(kblk_s, 1)

                def output(d):
                    step(f"o{d}")
                    act.activation(L4[:, d, :], slot(STEP[f"o{d}"])[:, 0:T], ACT.Copy)
                    freed(act.activation(sqo[d], slot(STEP[f"o{d}"])[:, 0:T], ACT.Square), f"o{d}")
                    act.drain().then_inc(o_sq, 1)

                def turn_v(d):
                    step(f"v{d}")
                    s = slot(STEP[f"v{d}"])
                    act.activation(v_t[:, 0:NC, d * P:(d + 1) * P], s[:, 0:TP].rearrange("p (c v) -> p c v", c=NC), ACT.Copy)
                    ins = act.activation(v_t[0:TS, NC, d * P:(d + 1) * P], s[0:TS, TP:TP + P], ACT.Copy)
                    freed(ins, f"v{d}")

                act.preload_act_table_set("natural_log_exp_and_others")
                for n in range(NU):
                    if n == 10:
                        act.preload_act_table_set("sigmoid_and_others")
                    hold(w_raw[(n + 3) % NRAW], loaded(n + 3, j * (NU // NRAW)))
                    hold(unit_done, j18 + (n + 1))
                    split_hi(n + 3)
                    if n >= 1:
                        evacuate(n - 1)
                    if n == 2:
                        hold(lbj_s, j * 3 + 3)
                        step("decay")
                        freed(act.activation(halves(Z[:, 0, :]), slot(STEP["decay"]).rearrange("p (a b) -> p a b", a=2)[:, :, 0:HT],
                                             ACT.Identity, bias=blr[:, :]), "decay")
                        act.drain()
                        act.activation(T3[:, :, :], Z[:, :, :], ACT.Abs)
                        act.drain()
                        act.activation(T3[:, :, :], T3[:, :, :], ACT.Exp, scale=-1.0)
                        act.drain()
                        act.activation(T3[:, :, :], T3[:, :, :], ACT.Ln, bias=one_c[:, :]).then_inc(z_abs, 1)
                    if n == 4:
                        hold(l_dve, j + 1)
                        act.activation(Z[:, 0, :], L4[:, 0, :], ACT.Exp, scale=1.0 / TAU)
                        for h in range(2):
                            act.activation(Z[:, 1 + h, :], L4[:, 1 + h, :], ACT.Exp, bias=lbj[:, 0, h:h + 1])
                            act.activation(K[:, 1 + h, :], K[:, 1 + h, :], ACT.Exp, bias=lbj[:, 0, h:h + 1])
                        act.drain().then_inc(l2_act, 1)
                    if n == 6:
                        act.drain().then_inc(qk_in, 1)
                    if 8 <= n < 12:
                        turn_v(n - 8)
                    if 7 <= n <= 10:
                        act.drain().then_inc(v_in, 1)
                    if n > GATE0 and (n - GATE0) % 2 == 0:
                        act.drain().then_inc(gate_in, 1)
                    if n == 15:
                        step("kt0")
                        freed(act.activation(k_flat[:, 0:8 * P], slot(STEP["kt0"]), ACT.Copy), "kt0")
                        step("kt1")
                        act.activation(k_flat[:, 8 * P:12 * P], slot(STEP["kt1"])[:, 0:4 * P], ACT.Copy)
                        freed(act.activation(k_flat[0:TS, 12 * P:15 * P], slot(STEP["kt1"])[0:TS, 4 * P:7 * P], ACT.Copy), "kt1")
                        act.drain().then_inc(k_tok, 1)
                        spread(0)
                    if n == 16:
                        hold(dec_s, j + 1)
                        spread(1)
                    if n == 17:
                        for d in range(3):
                            output(d)
                evacuate(NU - 1)
                act.drain().then_inc(gate_in, 1)
                output(3)
                step("ss1")
                spread(2)
                act.preload_act_table_set("natural_log_exp_and_others")
                for h in range(3):
                    step(f"norm{h}")
                    freed(act.activation(B[:, h, :], slot(STEP[f"norm{h}"])[:, 0:T], ACT.Ln,
                                         scale=1.0 / (DVG if h == 0 else P), bias=eps_c[:, :]), f"norm{h}")
                    act.drain()
                    act.activation(B[:, h, :], B[:, h, :], ACT.Exp, scale=-0.5).then_inc(rst, 1)

        @block.vector
        def _(dve):
            dve.memset(eps_c[:, :], EPS)
            dve.memset(one_c[:, :], 1.0)
            dve.memset(stat[:, :, :], 1.0).then_inc(setup, 1)
            dve.drain().then_inc(w_lo, 1)
            dve.drain().then_inc(unit_free, 1)
            dve.drain().then_inc(step_free[0], 1)
            dve.drain().then_inc(step_free[1], 1)
            dve.drain().then_inc(gate_s, 1)
            dve.drain().then_inc(merged_s, 1)
            dve.wait_ge(small, 16 * 6)
            dve.tensor_tensor(lb[:, 1, :], gain[:, 2, :], gain[:, 2, :], ALU.subtract).then_inc(lb_d, 1)
            dve.wait_ge(lb_a, 1)
            dve.reciprocal(lb[:, 2, :], lb[:, 1, :])
            dve.drain()
            dve.tensor_tensor(lb[:, 1, :], lb[:, 1, :], lb[:, 2, :], ALU.mult)
            dve.drain()
            dve.tensor_tensor(lb[:, 3, :], lb[:, 1, :], lb[:, 1, :], ALU.subtract)
            dve.drain()
            dve.tensor_scalar(lb[:, 5, :], lb[:, 3, :], 0.0, 1.0 - 1e-6, ALU.max, ALU.min)
            dve.drain()
            dve.tensor_scalar(lb[:, 4, :], lb[:, 5, :], 1e-20, None, ALU.max).then_inc(lb_d, 1)
            dve.wait_ge(lb_a, 2)
            dve.wait_ge(squared, 1)
            for c in range(NT):
                dve.tensor_scalar(xt[c][0:tok(c), :], xt[c][0:tok(c), :], stat[0:tok(c), 1, c:c + 1], None, ALU.mult).then_inc(scaled, 1)
            for k in range(KT):
                dve.wait_ge(x_hi_s, k + 1)
                dve.scalar_tensor_tensor(x_lo[:, k, :], turn_slot(ps, k)[:, 0:T], gain[:, 0, k:k + 1],
                                         x_hi[:, k, :].bitcast(F32), ALU.mult, ALU.subtract).then_inc(x_lo_s, 1)
            for u in range(3):
                dve.wait_ge(w_hi, u + 1)
                split_lo(u)
            dve.wait_ge(consts, CONSTS)
            with nc.vector.Fori(0, G) as j:
                j18 = dve.snap(j * NU)
                jr = dve.snap(j * NR)

                def step(name):
                    dve.wait_ge(step_done, jr + (STEP[name] + 1))

                def freed(ins, name):
                    ins.then_inc(step_free[STEP[name] % 2], 1)

                def blocks_of(t, L):
                    if L > SL:
                        return t[:, :, 0:TP].rearrange("p h (n b) -> p h n b", b=L)
                    return t[:, :, :].rearrange("p h (n b) -> p (h n) b", b=L)

                def block_decays():
                    for L in LEVELS:
                        n = over[2 * L].shape[2]
                        two = over[L][:, :, 0:2 * n].rearrange("p h (n b) -> p h n b", b=2)
                        dve.tensor_tensor(over[2 * L].rearrange("p h (n o) -> p h n o", o=1), two[:, :, :, 0:1], two[:, :, :, 1:2], ALU.mult)
                        dve.drain()
                    dve.tensor_copy(dec[:, :, 0:NC], over[C])
                    dve.tensor_copy(dec[:, :, NC:NC + NB], over[SL][:, :, TP // SL:T // SL]).then_inc(dec_s, 1)

                def level_next(i):
                    step(f"level{i}")
                    L = LEVELS[i]
                    q, k = blocks_of(Q, 2 * L), blocks_of(K, 2 * L)
                    if 2 * L > SL:
                        n = TP // (2 * L)
                        two = over[L][:, :, 0:2 * n].rearrange("p h (n b) -> p h n b", b=2)
                        shape = [P, 3, n, L]
                        kf, qf = k[:, :, :, 0:L], q[:, :, :, L:2 * L]
                        first, behind = two[:, :, :, 0:1], two[:, :, :, 1:2]
                    else:
                        two = over[L].rearrange("p h (n b) -> p (h n) b", b=2)
                        shape = [P, 3 * T // (2 * L), L]
                        kf, qf = k[:, :, 0:L], q[:, :, L:2 * L]
                        first, behind = two[:, :, 0:1], two[:, :, 1:2]
                    dve.tensor_tensor(qf, qf, first.broadcast_to(shape), ALU.mult)
                    ins = dve.tensor_tensor(kf, kf, behind.broadcast_to(shape), ALU.mult)
                    ins.then_inc(lvl if i < NL - 1 else qs, 1)

                def level_take(i):
                    dve.drain()
                    step(f"level{i}")
                    dve.memset(tick[:, :], 0.0)
                    L = LEVELS[i]
                    s = slot(STEP[f"level{i}"])
                    n = C // 2 // L
                    m = mask[:, i, :].bitcast(I32).rearrange("p (o a r) -> p o a r", o=1, r=L)
                    ins = dve.copy_predicated(
                        Am[:, :, :].rearrange("p h (a b) -> p h a b", b=2 * L)[:, :, :, L:2 * L],
                        m.broadcast_to([P, 3 * NC, n, L]),
                        s[:, 0:3 * NC * C // 2].rearrange("p (h a r) -> p h a r", a=n, r=L))
                    if L <= 4:
                        n = TS // 2 // L
                        o = 3 * NC * C // 2
                        ins = dve.copy_predicated(
                            As[:, :, :].rearrange("p h (a b) -> p h a b", b=2 * L)[:, :, :, L:2 * L],
                            m[0:TS, :, 0:n, :].broadcast_to([TS, 3, n, L]),
                            s[0:TS, o:o + 3 * TS // 2].rearrange("p (h a r) -> p h a r", a=n, r=L))
                    freed(ins, f"level{i}")

                def diagonal(i):
                    step(f"diag{i}")
                    s = slot(STEP[f"diag{i}"])
                    if i < 2:
                        ins = dve.tensor_tensor(Am[:, 6 * i:6 * i + 6, :], s[:, 0:6 * C].rearrange("p (h t) -> p h t", t=C),
                                                ident[:, :].rearrange("p (o t) -> p o t", o=1).broadcast_to([P, 6, C]), ALU.mult)
                    else:
                        ins = dve.tensor_tensor(As[:, :, :], s[0:TS, 0:3 * TS].rearrange("p (h t) -> p h t", t=TS),
                                                ident[0:TS, 0:TS].rearrange("p (o t) -> p o t", o=1).broadcast_to([TS, 3, TS]), ALU.mult)
                    freed(ins, f"diag{i}")

                def gate(t):
                    dve.wait_ge(gate_in, j * 4 + (t + 1))
                    dve.tensor_tensor(E2[:, 0, :], E2[:, 0, :], E2[:, 1, :], ALU.mult)
                    dve.drain()
                    dve.tensor_tensor(Gt[:, t, :], Gt[:, t, :], E2[:, 0, :], ALU.mult).then_inc(gate_s, 1)

                dve.tensor_copy(blr[:, :], blr4[:, bass.ds(j, 1)]).then_inc(lbj_s, 1)
                for a, b in ((0, 5), (1, 4)):
                    dve.tensor_copy(lbj[:, a, :], lb[:, b, bass.ds(2 * j, 2)]).then_inc(lbj_s, 1)
                dve.drain()
                for n in range(NU):
                    if 8 <= n < 8 + NL:
                        level_next(n - 8)
                    dve.wait_ge(w_hi, j18 + (n + 4))
                    split_lo(n + 3)
                    if n == 3:
                        dve.wait_ge(z_abs, j + 1)
                        dve.scalar_tensor_tensor(L4[:, 0:3, :], Z[:, :, :], 0.0, T3[:, :, :], ALU.min, ALU.subtract)
                        dve.drain()
                        dve.tensor_tensor(K[:, 1:3, :], L4[:, 1:3, :], Z[:, 1:3, :], ALU.subtract).then_inc(l_dve, 1)
                    if n == 5:
                        dve.wait_ge(l2_act, j + 1)
                        for h in range(2):
                            dve.tensor_scalar(Z[:, 1 + h, :], Z[:, 1 + h, :], lbj[:, 1, h:h + 1], None, ALU.add)
                        dve.drain()
                        block_decays()
                    if n == 7:
                        diagonal(0)
                        diagonal(1)
                        diagonal(2)
                        dve.tensor_tensor(Q[:, :, :], Q[:, :, :], Z[:, :, :], ALU.mult).then_inc(lvl, 1)
                    if 8 <= n < 8 + NL:
                        level_take(n - 8)
                    if n == 7 + NL:
                        dve.drain().then_inc(a_s, 1)
                    if n > GATE0 and (n - GATE0) % 2 == 0:
                        gate((n - GATE0) // 2 - 1)
                    if n == 16:
                        for i in range(2):
                            dve.drain()
                            step(f"ds{i}")
                            s = slot(STEP[f"ds{i}"])
                            for c in (2 * i, 2 * i + 1):
                                dS = s[:, (c % 2) * 4 * P:(c % 2 + 1) * 4 * P]
                                if c == 0:
                                    ins = dve.tensor_copy(sp_t[:, 0, :], dS)
                                else:
                                    if c != 2:
                                        dve.drain()
                                    for h, (a, b) in enumerate(((0, 256), (256, 384), (384, 512))):
                                        ins = dve.scalar_tensor_tensor(sp_t[:, c, a:b], sp_t[:, c - 1, a:b], dec[:, h, c:c + 1],
                                                                       dS[:, a:b], ALU.mult, ALU.add)
                            freed(ins, f"ds{i}")
                            dve.drain().then_inc(sp_s, 1)
                gate(3)
                for i in range(4):
                    step(f"ss{i}")
                    h = (0, 0, 1, 2)[i]
                    w = DVG if h == 0 else P
                    for b in (range(4 * i, 4 * i + 4) if i < 2 else range(NB)):
                        st = ssg[:, b, :] if h == 0 else ssh[:, b, h - 1, :]
                        ins = dve.scalar_tensor_tensor(st, st, dec[:, h, NC + b:NC + b + 1],
                                                       slot(STEP[f"ss{i}"])[:, (b * w) % 1024:(b * w) % 1024 + w], ALU.mult, ALU.add)
                    freed(ins, f"ss{i}")
                    dve.drain().then_inc(ss_s, 1)
                for h in range(3):
                    dve.wait_ge(rst, j * 3 + (h + 1))
                    for d in ((0, 1), (2,), (3,))[h]:
                        dve.scalar_tensor_tensor(L4[:, d, :], L4[:, d, :], onm[:, min(d, 2):min(d, 2) + 1], B[:, h, :], ALU.mult, ALU.mult)
                        dve.drain()
                        dve.tensor_tensor(L4[:, d, :], L4[:, d, :], Gt[:, d, :], ALU.mult)
                dve.drain()
                dve.tensor_tensor(merged[:, bass.ds(2 * j, 2), :], L4[:, 0:2, :], L4[:, 2:4, :], ALU.add).then_inc(merged_s, 1)

        @block.tensor
        def _(pe):
            pe.wait_ge(consts, CONSTS)
            for k in range(KT):
                if k >= 4:
                    pe.wait_ge(x_lo_s, k - 3)
                for c in range(NT):
                    if k == 0:
                        pe.wait_ge(scaled, c + 1)
                    m = nc.tensor.transpose(turn_slot(ps, k)[:, c * P:c * P + tok(c)], xt[c][0:tok(c), k * P:(k + 1) * P],
                                            ident[0:tok(c), 0:tok(c)])
                m.then_inc(turned, 1)
            pe.wait_ge(x_lo_s, KT)
            pe.wait_ge(w_lo, 2)
            unit_passes(0, proj(0), xh, xl).then_inc(unit_done, 1)
            pe.wait_ge(unit_free, 2)
            with nc.tensor.Fori(0, G) as j:
                j18 = pe.snap(j * NU)
                jh = pe.snap(j * (NR // 2))

                def taken(name):
                    pe.wait_ge(step_free[STEP[name] % 2], jh + (STEP[name] // 2 + 1))

                def do_step(name):
                    r = STEP[name]
                    s = slot(r)
                    taken(name)
                    if name == "decay":
                        pe.wait_ge(grp_in, j * 16 + 16)
                        for q in range(2):
                            m = nc.tensor.matmul(s[:, q * 512:q * 512 + HT], wlr[:, :], glr[:, q * HT:(q + 1) * HT], start=True, stop=True)
                    elif name[0] == "v":
                        d = int(name[1:])
                        pe.wait_ge(v_in, j * 4 + (d + 1))
                        for c in range(NT):
                            m = nc.tensor.transpose(s[0:tok(c), c * P:(c + 1) * P], Gt[:, d, c * P:c * P + tok(c)], ident[:, :])
                    elif name[:4] == "diag":
                        i = int(name[4:])
                        if i == 0:
                            pe.wait_ge(qk_in, j + 1)
                        for a in range(6 if i < 2 else 0):
                            c, h = divmod(6 * i + a, 3)
                            m = nc.tensor.matmul(s[:, a * C:(a + 1) * C], K[:, h, c * C:(c + 1) * C], Q[:, h, c * C:(c + 1) * C],
                                                 start=True, stop=True)
                        if i == 2:
                            for h in range(3):
                                m = nc.tensor.matmul(s[0:TS, h * TS:(h + 1) * TS], K[:, h, TP:T], Q[:, h, TP:T],
                                                     start=True, stop=True)
                    elif name[:5] == "level":
                        i = int(name[5:])
                        L = LEVELS[i]
                        pe.wait_ge(lvl, j * NL + (i + 1))
                        for a in range(3 * NC):
                            c, h = divmod(a, 3)
                            m = nc.tensor.matmul(s[:, a * C // 2:(a + 1) * C // 2], K[:, h, c * C:(c + 1) * C], second(Q[:, h, c * C:(c + 1) * C], L),
                                                 start=True, stop=True)
                        if L <= 4:
                            for h in range(3):
                                o = 3 * NC * C // 2 + h * TS // 2
                                m = nc.tensor.matmul(s[0:TS, o:o + TS // 2], K[:, h, TP:T], second(Q[:, h, TP:T], L), start=True, stop=True)
                    elif name[:2] == "kt":
                        i = int(name[2:])
                        if i == 0:
                            pe.wait_ge(qs, j + 1)
                        for a in (range(8) if i == 0 else range(8, 3 * NT)):
                            c, h = divmod(a, 3)
                            m = nc.tensor.transpose(s[0:tok(c), (a % 8) * P:(a % 8 + 1) * P], K[:, h, c * P:c * P + tok(c)], ident[:, :])
                    elif name[:2] == "ds":
                        i = int(name[2:])
                        pe.wait_ge(k_tok, j + 1)
                        for c in (2 * i, 2 * i + 1):
                            for h, (a, b) in enumerate(((0, 256), (256, 384), (384, 512))):
                                o = (c % 2) * 512
                                m = nc.tensor.matmul(s[:, o + a:o + b], k_t[:, c, h * P:(h + 1) * P], v_t[:, c, a:b], start=True, stop=True)
                    elif name[0] == "o":
                        d = int(name[1:])
                        h = head_of[d]
                        cols = slice(d * P, (d + 1) * P)
                        if d == 0:
                            pe.wait_ge(a_s, j + 1)
                            pe.wait_ge(sp_s, j * 2 + 2)
                            pe.wait_ge(st_in, j * 48 + 48)
                        for c in range(NC):
                            m = nc.tensor.matmul(s[:, c * C:(c + 1) * C], v_t[:, c, cols], Am[:, 3 * c + h, :], start=True, stop=(c == 0))
                            if c > 0:
                                m = nc.tensor.matmul(s[:, c * C:(c + 1) * C], sp_t[:, c - 1, cols], Q[:, h, c * C:(c + 1) * C],
                                                     start=False, stop=True)
                        for b in range(NB):
                            st = ssg[:, b, cols] if d < 2 else ssh[:, b, d - 2, :]
                            nc.tensor.matmul(s[:, TP + b * SL:TP + (b + 1) * SL], st, Q[:, h, TP + b * SL:TP + (b + 1) * SL],
                                             start=(b == 0), stop=False, skip_group_check=True)
                        m = nc.tensor.matmul(s[:, TP:T], v_t[0:TS, NC, cols], As[:, h, :], start=False, stop=True, skip_group_check=True)
                    elif name[:4] == "norm":
                        h = int(name[4:])
                        pe.wait_ge(o_sq, j * 4 + (2, 3, 4)[h])
                        for a, b in ((0, TP), (TP, T)):
                            for d in ((0, 1), (2,), (3,))[h]:
                                m = nc.tensor.matmul(s[:, a:b], ones[:, :], sqo[d][:, a:b], start=(d in (0, 2, 3)), stop=(d in (1, 2, 3)))
                    elif name[:2] == "ss":
                        i = int(name[2:])
                        pe.wait_ge(kblk_s, j * 3 + (1, 1, 2, 3)[i])
                        for b in (range(4 * i, 4 * i + 4) if i < 2 else range(NB)):
                            if i < 2:
                                o, v = (b % 4) * DVG, v_t[0:TS, NC, 0:DVG]
                            else:
                                o, v = b * P, v_t[0:TS, NC, i * P:(i + 1) * P]
                            m = nc.tensor.matmul(s[:, o:o + v.shape[-1]], kblk[(0, 0, 1, 2)[i]][:, b, :], v, start=True, stop=True)
                    m.then_inc(step_done, 1)

                for n in range(NU):
                    pe.wait_ge(unit_free, j18 + (n + 1))
                    pe.wait_ge(w_lo, j18 + (n + 3))
                    unit_passes(n + 1, proj(n + 1), xh, xl).then_inc(unit_done, 1)
                    for name in AFTER.get(n, []):
                        do_step(name)
    sa.close()

    so = ExitStack()
    sbk = ExitStack()
    g_post = sb("g_post", [P, D], F32, sbk)
    mt = sb("mt", [P, KT, T], F32, sbk)
    hn = sb("hn", [P, 2, D], F32, sbk)
    msq = sb("msq", [P, D], F32, sbk)
    h_in = sem("h_in")
    m_hi = sem("m_hi")
    m_lo = sem("m_lo")
    mt_s = sem("mt_s")
    m_tok = sem("m_tok")
    m_rms = sem("m_rms")
    m_half = sem("m_half")
    h_s = sem("h_s")
    h_rms = sem("h_rms")
    hn_s = sem("hn_s")
    h_turn = sem("h_turn")
    f_hi = sem("f_hi")
    f_lo = sem("f_lo")
    with nc.Block() as block:
        @block.sync
        def _(sp):
            sp.wait_ge(st_out, 80 * G)
            for c in range(NT):
                sp.dma_start(h_t[0:tok(c), c, :], xp_v[c] if c < NC else xs_v).then_inc(h_in, 16)
            sp.dma_start(g_post[:, :], norm_mix_post.partition_broadcast(P).rearrange("p o d -> p (o d)")).then_inc(h_in, 16)
            for u in range(UB + 2, UC + 2):
                sp.wait_ge(w_lo, u)
                src = wout_v[:, :, (u - UB) * P:(u - UB + 1) * P] if u < UC else wf1_v[:, :, (u - UC) * FF:(u - UC) * FF + P]
                load_unit(sp, u, src)

        @block.scalar
        def _(act):
            for k in range(KT):
                act.activation(x_hi[:, k, :], merged[:, k, :], ACT.Copy).then_inc(m_hi, 1)
            for u in range(UB, UC):
                act.wait_ge(w_raw[(u + 2) % NRAW], loaded(u + 2))
                act.wait_ge(unit_done, u)
                split_hi(u + 2)
                act.wait_ge(unit_done, u + 1)
                act.activation(halves(mt[:, u - UB, :]), proj(u), ACT.Copy).then_inc(unit_free, 1)
            for c in range(NT):
                n = tok(c)
                act.wait_ge(m_tok, c + 1)
                act.drain()
                act.activation(msq[0:n, :], tok_slot(ps, c)[0:n, :], ACT.Square, accum_out=stat[0:n, 0, c:c + 1])
                act.drain()
                act.activation(stat[0:n, 1, c:c + 1], stat[0:n, 0, c:c + 1], ACT.Ln, scale=1.0 / D, bias=eps_c[0:n, :])
                act.drain()
                act.activation(stat[0:n, 1, c:c + 1], stat[0:n, 1, c:c + 1], ACT.Exp, scale=-0.5).then_inc(m_rms, 1)
                act.wait_ge(h_s, c + 1)
                act.activation(msq[0:n, :], h_t[0:n, c, :], ACT.Square, accum_out=stat[0:n, 0, c:c + 1])
                act.drain()
                act.activation(stat[0:n, 1, c:c + 1], stat[0:n, 0, c:c + 1], ACT.Ln, scale=1.0 / D, bias=eps_c[0:n, :])
                act.drain()
                act.activation(stat[0:n, 1, c:c + 1], stat[0:n, 1, c:c + 1], ACT.Exp, scale=-0.5).then_inc(h_rms, 1)
                act.wait_ge(h_turn, c + 1)
                for q in range(2):
                    s = tok_slot(ps, c)[:, q * 512:(q + 1) * 512].rearrange("p (k t) -> p k t", k=4)
                    for k in range(4):
                        ins = act.activation(x_hi[:, 4 * q + k, c * P:c * P + n], s[:, k, 0:n], ACT.Copy,
                                             scale=gain[:, 1, 4 * q + k:4 * q + k + 1])
                ins.then_inc(f_hi, 1)

        @block.vector
        def _(dve):
            for k in range(KT):
                dve.wait_ge(m_hi, k + 1)
                dve.tensor_tensor(x_lo[:, k, :], merged[:, k, :], x_hi[:, k, :].bitcast(F32), ALU.subtract).then_inc(m_lo, 1)
            for u in range(UB, UC):
                dve.wait_ge(w_hi, u + 3)
                split_lo(u + 2)
            dve.wait_ge(h_in, 16 * (NT + 1))
            for c in range(NT):
                n = tok(c)
                dve.wait_ge(m_rms, c + 1)
                if c >= 2:
                    dve.wait_ge(h_turn, c - 1)
                dve.scalar_tensor_tensor(hn[0:n, c % 2, :], tok_slot(ps, c)[0:n, :], stat[0:n, 1, c:c + 1], g_post[0:n, :],
                                         ALU.mult, ALU.mult).then_inc(m_half, 1)
                dve.drain()
                dve.tensor_tensor(h_t[0:n, c, :], h_t[0:n, c, :], hn[0:n, c % 2, :], ALU.add).then_inc(h_s, 1)
                dve.wait_ge(h_rms, c + 1)
                dve.tensor_scalar(hn[0:n, c % 2, :], h_t[0:n, c, :], stat[0:n, 1, c:c + 1], None, ALU.mult).then_inc(hn_s, 1)
                dve.wait_ge(f_hi, c + 1)
                for q in range(2):
                    s = tok_slot(ps, c)[:, q * 512:(q + 1) * 512].rearrange("p (k t) -> p k t", k=4)
                    for k in range(4):
                        ins = dve.scalar_tensor_tensor(x_lo[:, 4 * q + k, c * P:c * P + n], s[:, k, 0:n],
                                                       gain[:, 1, 4 * q + k:4 * q + k + 1],
                                                       x_hi[:, 4 * q + k, c * P:c * P + n].bitcast(F32), ALU.mult, ALU.subtract)
                ins.then_inc(f_lo, 1)

        @block.tensor
        def _(pe):
            for u in range(UB, UC):
                pe.wait_ge(unit_free, u)
                pe.wait_ge(w_lo, u + 2)
                if u == UB:
                    pe.wait_ge(m_lo, KT)
                unit_passes(u, proj(u), xh, xl).then_inc(unit_done, 1)

            def turn_m(c):
                if c >= 4:
                    pe.wait_ge(f_lo, c - 3)
                for k in range(KT):
                    m = nc.tensor.transpose(tok_slot(ps, c)[0:tok(c), k * P:(k + 1) * P], mt[:, k, c * P:c * P + tok(c)], ident[:, :])
                m.then_inc(m_tok, 1)

            pe.wait_ge(unit_free, UC + 1)
            for c in range(4):
                turn_m(c)
            for c in range(NT):
                n = tok(c)
                if c == 4:
                    turn_m(4)
                pe.wait_ge(m_half, c + 1)
                pe.wait_ge(hn_s, c + 1)
                for k in range(KT):
                    m = nc.tensor.transpose(tok_slot(ps, c)[:, k * P:k * P + n], hn[0:n, c % 2, k * P:(k + 1) * P], ident[0:n, 0:n])
                m.then_inc(h_turn, 1)
    sbk.close()
    merged_stack.close()

    act_hi = sb("act_hi", [P, FT, T], F32R)
    act_lo = sb("act_lo", [P, FT, T], F32R)
    sc = ExitStack()
    fe = sb("fe", [P, 2, T], F32, sc)
    fa = sb("fa", [P, 2, T], F32, sc)
    hs_out = sem("hs_out")
    ff_a = sem("ff_a")
    ff_d = sem("ff_d")
    ff_h = sem("ff_h")
    ff_l = sem("ff_l")
    PAIRS = 3
    LOOPS = (FT - 1) // PAIRS
    with nc.Block() as block:
        @block.sync
        def _(sp):
            sp.dma_start(ys_v, h_t[0:TS, NC, :]).then_inc(hs_out, 16)
            with nc.sync.Fori(0, LOOPS) as i:
                i6 = sp.snap(i * 2 * PAIRS)
                for n in range(2 * PAIRS):
                    first = sp.snap(i * (PAIRS * P) + ((n // 2 + 1) * P + n % 2 * FF))
                    sp.wait_ge(w_lo, i6 + (UC + 2 + n))
                    load_unit(sp, UC + 2 + n, wf1_v[:, :, bass.ds(first, P)])
            for n in range(2):
                sp.wait_ge(w_lo, UD + n)
                load_unit(sp, UD + n, wf2_v[:, KCUT[n][0]:KCUT[n][0] + KCUT[n][1], 0:P], KCUT[n][1])

        @block.scalar
        def _(act):
            scratch = act.alloc_register("act_scratch_c")
            act.reg_mov(scratch, 0)

            def pair(i6, i3, p):
                for n in (2 * p, 2 * p + 1):
                    held(act, scratch, w_raw[(UC + n + 2) % NRAW], loaded(UC + n + 2, i3))
                    held(act, scratch, unit_done, i6 + (UC + n))
                    split_hi(UC + n + 2, KT)
                    held(act, scratch, unit_done, i6 + (UC + n + 1))
                    if n % 2 == 0:
                        held(act, scratch, ff_l, i3 + (p + 1))
                        act.activation(halves(fe[:, 0, :]), proj(UC + n), ACT.Sigmoid)
                        act.activation(halves(fa[:, 0, :]), proj(UC + n), ACT.Copy).then_inc(unit_free, 1)
                        act.drain().then_inc(ff_a, 1)
            with nc.scalar.Fori(0, LOOPS) as i:
                i6 = act.snap(i * 2 * PAIRS)
                i3 = act.snap(i * PAIRS)
                for p in range(PAIRS):
                    pair(i6, i3, p)
            pair(2 * PAIRS * LOOPS, PAIRS * LOOPS, 0)

        @block.vector
        def _(dve):
            dve.memset(fe[:, :, 0:1], 0.0).then_inc(ff_l, 1)

            def pair(i6, i3, p, row):
                for n in (2 * p, 2 * p + 1):
                    dve.wait_ge(w_hi, i6 + (UC + n + 3))
                    split_lo(UC + n + 2)
                dve.wait_ge(ff_a, i3 + (p + 1))
                dve.tensor_tensor(fa[:, 0, :], fa[:, 0, :], fe[:, 0, :], ALU.mult)
                dve.drain()
                dve.wait_ge(unit_done, i6 + (UC + 2 * p + 2))
                dve.tensor_tensor(halves(fe[:, 0, :]), halves(fa[:, 0, :]), proj(UC + 2 * p + 1), ALU.mult).then_inc(unit_free, 1)
                dve.drain()
                dve.tensor_copy(act_hi[:, row, :], fe[:, 0:1, :])
                dve.drain()
                dve.tensor_tensor(act_lo[:, row, :], fe[:, 0:1, :], act_hi[:, row, :].bitcast(F32), ALU.subtract).then_inc(ff_l, 1)
            with nc.vector.Fori(0, LOOPS) as i:
                i6 = dve.snap(i * 2 * PAIRS)
                i3 = dve.snap(i * PAIRS)
                for p in range(PAIRS):
                    pair(i6, i3, p, bass.ds(i * PAIRS + p, 1))
            pair(2 * PAIRS * LOOPS, PAIRS * LOOPS, 0, slice(FT - 1, FT))

        @block.tensor
        def _(pe):
            def pair(i6, p):
                for n in (2 * p, 2 * p + 1):
                    pe.wait_ge(unit_free, i6 + (UC + n))
                    pe.wait_ge(w_lo, i6 + (UC + n + 2))
                    unit_passes(UC + n, proj(UC + n), xh, xl).then_inc(unit_done, 1)
            with nc.tensor.Fori(0, LOOPS) as i:
                i6 = pe.snap(i * 2 * PAIRS)
                for p in range(PAIRS):
                    pair(i6, p)
            pair(2 * PAIRS * LOOPS, 0)
    sc.close()

    f_t = sb("f_t", [P, T])
    f_main = sb("f_main", [P, NC, D])
    f_tok = [f_main[:, c, :] for c in range(NC)] + [h_t[:, NC, :]]
    h_back = w_raw_t[:, 1, :, :].rearrange("p k n -> p (k n)")
    h_tok = [h_t[:, c, :] for c in range(NC)] + [h_back]
    g_last = w_raw_t[:, 0, :, :].rearrange("p k n -> p (k n)")
    g_in = sem("g_in")
    ft_s = sem("ft_s")
    ft_turn = sem("ft_turn")
    ft_tok = sem("ft_tok")
    y_rms = sem("y_rms")
    y_s = sem("y_s")
    y_out = sem("y_out")
    TILES = 2
    NCUT = len(KCUT)
    BODY = TILES * NCUT
    LOOPD = KT // TILES
    with nc.Block() as block:
        def g_sq(c, n):
            return ps[0:n, 0:2, :].rearrange("p a b -> p (a b)")

        @block.sync
        def _(sp):
            def loads(i6, col, ns):
                for n in ns:
                    k0, nk = KCUT[n % NCUT]
                    where = col(n // NCUT)
                    sp.wait_ge(w_lo, i6 + (UD + n))
                    load_unit(sp, UD + n, wf2_v[:, k0:k0 + nk, where], nk)
            with nc.sync.Fori(0, LOOPD - 1) as i:
                i6 = sp.snap(i * BODY)
                loads(i6, lambda t: bass.ds(sp.snap(i * (TILES * P) + t * P), P), range(2, BODY + 2))
            i6 = (LOOPD - 1) * BODY
            loads(i6, lambda t: slice((LOOPD - 1) * TILES * P + t * P, (LOOPD - 1) * TILES * P + (t + 1) * P), range(2, BODY))
            sp.wait_ge(hs_out, 16)
            sp.wait_ge(w_lo, UD + KT * NCUT + 1)
            sp.dma_start(g_last, norm_ffn_post.partition_broadcast(P).rearrange("p o d -> p (o d)")).then_inc(g_in, 16)
            sp.dma_start(h_back[0:TS, :], ys_v).then_inc(g_in, 16)
            sp.wait_ge(g_in, 32)
            for c in range(NT):
                sp.wait_ge(y_s, c + 1)
                sp.dma_start(yp_v[c] if c < NC else ys_v, f_tok[c][0:tok(c), :]).then_inc(y_out, 16)
            sp.wait_ge(y_out, 16 * NT)

        @block.gpsimd
        def _(pool):
            pool.wait_ge(st_out, 80 * G)

        @block.scalar
        def _(act):
            scratch = act.alloc_register("act_scratch_d")
            act.reg_mov(scratch, 0)

            def body(i6, i3, i2, last):
                for n in range(BODY):
                    if not last or n < BODY - 2:
                        held(act, scratch, w_raw[(UD + n + 2) % NRAW], loaded(UD + n + 2, i3))
                        held(act, scratch, unit_done, i6 + (UD + n))
                        split_hi(UD + n + 2, KCUT[(n + 2) % NCUT][1])
                    if n % NCUT == NCUT - 1:
                        m = n // NCUT
                        held(act, scratch, unit_done, i6 + (UD + n + 1))
                        held(act, scratch, ft_tok, i2 + (m + 2))
                        act.activation(halves(f_t[:, :]), proj(m), ACT.Copy).then_inc(ft_s, 1)
            with nc.scalar.Fori(0, LOOPD - 1) as i:
                body(act.snap(i * BODY), act.snap(i * (BODY // NRAW)), act.snap(i * TILES), False)
            body((LOOPD - 1) * BODY, (LOOPD - 1) * BODY // NRAW, (LOOPD - 1) * TILES, True)
            act.wait_ge(ft_tok, KT + 2)
            for c in range(NT):
                n = tok(c)
                act.activation(g_sq(c, n), f_tok[c][0:n, :], ACT.Square, accum_out=stat[0:n, 0, c:c + 1])
                act.drain()
                act.activation(stat[0:n, 1, c:c + 1], stat[0:n, 0, c:c + 1], ACT.Ln, scale=1.0 / D, bias=eps_c[0:n, :])
                act.drain()
                act.activation(stat[0:n, 1, c:c + 1], stat[0:n, 1, c:c + 1], ACT.Exp, scale=-0.5).then_inc(y_rms, 1)

        @block.vector
        def _(dve):
            for _ in range(2):
                dve.drain().then_inc(ft_tok, 1)

            def body(i6, i2, last, tile):
                for n in range(BODY):
                    if not last or n < BODY - 2:
                        dve.wait_ge(w_hi, i6 + (UD + n + 3))
                        split_lo(UD + n + 2, KCUT[(n + 2) % NCUT][1])
                    if n == NCUT + 1:
                        take(i2, 0, tile)
                take(i2, 1, tile)

            dve.wait_ge(hs_out, 16)

            def take(i2, m, tile):
                dve.wait_ge(ft_turn, i2 + (m + 1))
                s = slot(m)
                dve.tensor_copy(f_main[:, :, tile(m)], s[:, 0:TP].rearrange("p (c v) -> p c v", c=NC))
                dve.tensor_copy(f_tok[NC][0:TS, tile(m)], s[0:TS, TP:TP + P]).then_inc(ft_tok, 1)
            with nc.vector.Fori(0, LOOPD - 1) as i:
                body(dve.snap(i * BODY), dve.snap(i * TILES), False, lambda m: bass.ds(i * (TILES * P) + m * P, P))
            base = (LOOPD - 1) * TILES * P
            body((LOOPD - 1) * BODY, (LOOPD - 1) * TILES, True, lambda m: slice(base + m * P, base + (m + 1) * P))
            dve.wait_ge(g_in, 32)
            dve.drain()
            for c in range(NT):
                n = tok(c)
                dve.wait_ge(y_rms, c + 1)
                dve.scalar_tensor_tensor(f_tok[c][0:n, :], f_tok[c][0:n, :], stat[0:n, 1, c:c + 1], g_last[0:n, :], ALU.mult, ALU.mult)
                dve.drain()
                dve.tensor_tensor(f_tok[c][0:n, :], f_tok[c][0:n, :], h_tok[c][0:n, :], ALU.add).then_inc(y_s, 1)

        @block.tensor
        def _(pe):
            def turn(i2, m):
                pe.wait_ge(ft_s, i2 + (m + 1))
                for c in range(NT):
                    ins = nc.tensor.transpose(slot(m)[0:tok(c), c * P:(c + 1) * P], f_t[:, c * P:c * P + tok(c)], ident[:, :])
                ins.then_inc(ft_turn, 1)

            def body(i6, i2):
                for n in range(BODY):
                    m, cut = divmod(n, NCUT)
                    k0, nk = KCUT[cut]
                    pe.wait_ge(w_lo, i6 + (UD + n + 2))
                    if cut == 0:
                        pe.wait_ge(ft_tok, i2 + (m + 1))
                    unit_passes(UD + n, proj(m), lambda k, q: act_hi[:, k0 + k, q * HT:(q + 1) * HT],
                                lambda k, q: act_lo[:, k0 + k, q * HT:(q + 1) * HT], nk,
                                first=(cut == 0), last=(cut == NCUT - 1)).then_inc(unit_done, 1)
                    if m == 1 and cut == 0:
                        turn(i2, 0)
                turn(i2, 1)
            with nc.tensor.Fori(0, LOOPD - 1) as i:
                body(pe.snap(i * BODY), pe.snap(i * TILES))
            body((LOOPD - 1) * BODY, (LOOPD - 1) * TILES)
    keep.close()


CONSTS = 5 + 1 + 2 * NL + 2
SETUP = 1


def turn_slot(ps, k):
    return ps[:, 2 * (k % 4):2 * (k % 4) + 2, :].rearrange("p a b -> p (a b)")


def tok_slot(ps, c):
    return ps[:, 2 * (c % 4):2 * (c % 4) + 2, :].rearrange("p a b -> p (a b)")


_INS = ["x_prompt", "x_sample", "state_gla", "state_hgrn", "norm_mix_pre", "norm_mix_post", "norm_ffn_pre",
        "norm_ffn_post", "w_in", "gla_w_lr2", "gla_b_lr", "gla_onorm", "hgrn_lb", "hgrn_onorm", "w_out",
        "w_ffn_in", "w_ffn_out"]
_BY_FEATURE = ("norm_mix_pre", "norm_ffn_pre", "gla_b_lr", "gla_onorm", "hgrn_lb", "hgrn_onorm")
_OUTS = [((1, 512, 1024), "float32"), ((8, 8, 1024), "float32"), ((1, 1, 4, 128, 256), "float32"),
         ((1, 8, 4, 128, 256), "float32"), ((1, 1, 8, 128, 128), "float32"), ((1, 8, 8, 128, 128), "float32")]


def kernel(**inputs):
    import numpy as _np
    import concourse.bacc as _bacc
    from concourse import mybir as _mybir
    from concourse.bass_utils import run_bass_kernel_spmd as _run

    nc = _bacc.Bacc("TRN2", target_bir_lowering=False, num_devices=1)
    arrays, args = {}, []
    for name in _INS:
        a = inputs[name]
        if name in _BY_FEATURE:
            a = _np.asarray(a).reshape(-1, 128).T
        a = _np.ascontiguousarray(a)
        arrays[f"in_{name}_dram"] = a
        args.append(nc.dram_tensor(f"in_{name}_dram", a.shape, _mybir.dt.from_np(a.dtype), kind="ExternalInput").ap())
    for i, (shape, dtype) in enumerate(_OUTS):
        dt = _mybir.dt.from_np(_np.dtype(dtype))
        args.append(nc.dram_tensor(f"out_{i}_dram", shape, dt, kind="ExternalOutput").ap())
    build(nc, *args)
    r = _run(nc, [arrays], core_ids=[0])
    return tuple(r.results[0][f"out_{i}_dram"] for i in range(len(_OUTS)))
```

```python
from contextlib import ExitStack

import concourse.bass as bass
import concourse.mybir as mybir

ALU = mybir.AluOpType
ACT = mybir.ActivationFunctionType
F32 = mybir.dt.float32
F32R = mybir.dt.float32r
I32 = mybir.dt.int32

P = 128
D = 1024
KT = D // P
TP, NB, SL = 512, 8, 8
TS = NB * SL
T = TP + TS
HT = T // 2
C = 128
NC = TP // C
NT = NC + 1
GH, HH = 4, 8
GR, DVG = 16, 256
FF = 2816
FT = FF // P
EPS = 1e-6
TAU = 16.0
LEVELS = (1, 2, 4, 8, 16, 32, 64)
NL = len(LEVELS)
G = GH
ENDS = [0]
for _w in (512, 512, 1024, 1024, GR, 1024, 1024, 1024, 1024, 1024, 1024):
    ENDS.append(ENDS[-1] + _w)
GQ, GK, GV, GG, GLR, HQ, HF, HI, HG, GA, GB = ENDS[:-1]

UNITS = [(HF, 256, 0), (HF, 256, 1), (GK, 128, 0), (GQ, 128, 0), (HQ, 256, 0), (HQ, 256, 1),
         (GV, 256, 0), (GV, 256, 1), (HI, 256, 0), (HI, 256, 1),
         (GA, 256, 0), (GG, 256, 0), (GA, 256, 1), (GG, 256, 1),
         (GB, 256, 0), (HG, 256, 0), (GB, 256, 1), (HG, 256, 1)]
NU = len(UNITS)
GATE0 = 10
UB = 1 + G * NU
UC = UB + D // P
UD = UC + 2 * FT
KCUT = ((0, 8), (8, 8), (16, 6))
NRAW, NSPL = 2, 3

AFTER = {1: ["decay"], 6: ["diag0", "diag1", "diag2"], 7: ["level0", "v0"], 8: ["level1", "v1"], 9: ["level2", "v2"],
         10: ["level3", "v3"], 11: ["level4"], 12: ["level5"], 13: ["level6"], 14: ["kt0", "kt1"], 15: ["ds0", "ds1"],
         16: ["o0", "o1", "ss0", "o2"], 17: ["ss1", "o3", "ss2", "norm0", "norm1", "norm2", "ss3"]}
STEPS = [s for n in range(NU) for s in AFTER.get(n, [])]
NR = len(STEPS)
STEP = {name: r for r, name in enumerate(STEPS)}
assert NR % 2 == 0


def build(nc, x_prompt, x_sample, state_gla, state_hgrn, norm_mix_pre, norm_mix_post, norm_ffn_pre,
          norm_ffn_post, w_in, gla_w_lr2, gla_b_lr, gla_onorm, hgrn_lb, hgrn_onorm, w_out, w_ffn_in,
          w_ffn_out, y_prompt, y_sample, gla_prompt, gla_sample, hgrn_prompt, hgrn_sample):
    keep = ExitStack()

    def sb(name, shape, dt=F32, on=None):
        return (on or keep).enter_context(nc.sbuf_tensor(name, shape, dt))

    def sem(name):
        return keep.enter_context(nc.semaphore(name))

    x_hi = sb("x_hi", [P, KT, T], F32R)
    x_lo = sb("x_lo", [P, KT, T], F32R)
    w_raw_t = sb("w_raw_t", [P, NRAW, KT, P])
    w_hi_t = sb("w_hi_t", [P, NSPL, KT, P], F32R)
    w_lo_t = sb("w_lo_t", [P, NSPL, KT, P], F32R)
    ident = sb("ident", [P, P])
    eps_c = sb("eps_c", [P, 1])
    one_c = sb("one_c", [P, 1])
    gain = sb("gain", [P, 2, KT])
    stat = sb("stat", [P, 2, NT])
    h_t = sb("h_t", [P, NT, D])
    ps = keep.enter_context(nc.psum_tensor("ps", [P, 8, 512], F32))

    def proj(u):
        return ps[:, 2 * (u % 2):2 * (u % 2) + 2, 0:HT]

    def slot(r):
        return ps[:, 4 + 2 * (r % 2):6 + 2 * (r % 2), :].rearrange("p a b -> p (a b)")

    def halves(ap):
        return ap.rearrange("p (a b) -> p a b", a=2)

    w_raw = [sem(f"w_raw{i}") for i in range(NRAW)]
    w_hi = sem("w_hi")
    w_lo = sem("w_lo")
    unit_done = sem("unit_done")
    unit_free = sem("unit_free")
    step_done = sem("step_done")
    step_free = [sem("step_free0"), sem("step_free1")]
    small = sem("small")
    consts = sem("consts")
    setup = sem("setup")
    x_in = [sem(f"x_in{c}") for c in range(NT)]
    squared = sem("squared")
    scaled = sem("scaled")
    turned = sem("turned")
    x_hi_s = sem("x_hi_s")
    x_lo_s = sem("x_lo_s")
    lb_a = sem("lb_a")
    lb_d = sem("lb_d")
    st_in = sem("st_in")
    st_out = sem("st_out")
    lbj_s = sem("lbj_s")
    z_abs = sem("z_abs")
    l_dve = sem("l_dve")
    l2_act = sem("l2_act")
    qk_in = sem("qk_in")
    lvl = sem("lvl")
    qs = sem("qs")
    dec_s = sem("dec_s")
    a_s = sem("a_s")
    v_in = sem("v_in")
    k_tok = sem("k_tok")
    sp_s = sem("sp_s")
    kblk_s = sem("kblk_s")
    ss_s = sem("ss_s")
    gate_in = sem("gate_in")
    gate_s = sem("gate_s")
    o_sq = sem("o_sq")
    rst = sem("rst")
    merged_s = sem("merged_s")
    m_hi = sem("m_hi")

    v2 = lambda w: w.rearrange("o (k p) n -> p (o k) n", p=P)
    win_v, wout_v, wf1_v, wf2_v = v2(w_in), v2(w_out), v2(w_ffn_in), v2(w_ffn_out)
    xp_v = x_prompt.rearrange("o (c p) d -> c p (o d)", p=P)
    xs_v = x_sample.rearrange("b t d -> (b t) d")
    yp_v = y_prompt.rearrange("o (c p) d -> c p (o d)", p=P)
    ys_v = y_sample.rearrange("b t d -> (b t) d")
    tok = lambda c: P if c < NC else TS
    gla_v = lambda t: t.rearrange("o b h k v -> k (o b h) v").rearrange("k (b h) v -> k h b v", h=GH)
    hgrn_v = lambda t: t.rearrange("o b h k v -> k (o b h) v").rearrange("k (b h) v -> k h b v", h=HH)
    head = lambda t, i: t[:, bass.ds(i, 1), :, :].rearrange("k o b v -> k (o b) v")

    def held(eng, scratch, s, value):
        eng.wait_ge(s, value)
        eng.reg_alu(scratch, scratch, 1, ALU.add)

    def load_unit(eng, u, src, nk=KT):
        eng.dma_start(w_raw_t[:, u % NRAW, 0:nk, :], src).then_inc(w_raw[u % NRAW], 16)

    def loaded(u, more=0):
        return more * 16 + 16 * (u // NRAW + 1)

    def split_hi(u, nk=KT):
        nc.scalar.activation(w_hi_t[:, u % NSPL, 0:nk, :], w_raw_t[:, u % NRAW, 0:nk, :],
                             ACT.Copy).then_inc(w_hi, 1)

    def split_lo(u, nk=KT):
        nc.vector.tensor_tensor(w_lo_t[:, u % NSPL, 0:nk, :], w_raw_t[:, u % NRAW, 0:nk, :],
                                w_hi_t[:, u % NSPL, 0:nk, :].bitcast(F32), ALU.subtract).then_inc(w_lo, 1)

    def unit_passes(u, out, hi, lo, nk=KT, first=True, last=True, ready=None):
        todo = [(w, x, k) for k in range(nk) for w, x in ((w_lo_t, hi), (w_hi_t, lo), (w_hi_t, hi))]
        for i, (w, x, k) in enumerate(todo):
            if ready is not None and i % 3 == 0:
                ready(k)
            for q in range(2):
                m = nc.tensor.matmul(out[:, q, :], w[:, u % NSPL, k, :], x(k, q),
                                     start=first and i == 0, stop=last and i == len(todo) - 1)
        return m

    xh = lambda k, q: x_hi[:, k, q * HT:(q + 1) * HT]
    xl = lambda k, q: x_lo[:, k, q * HT:(q + 1) * HT]

    merged_stack = ExitStack()
    merged = sb("merged", [P, KT, T], F32, merged_stack)
    sa = ExitStack()
    A = lambda name, shape, dt=F32: sb(name, shape, dt, sa)
    Z = A("Z", [P, 3, T])
    L4 = A("L4", [P, 4, T])
    T3 = A("T3", [P, 3, T])
    B = A("B", [P, 3, T])
    Q = A("Q", [P, 3, T])
    K = A("K", [P, 3, T])
    Am = A("Am", [P, NC * 3, C])
    As = A("As", [TS, 3, TS])
    v_t = A("v_t", [P, NT, 4 * P])
    k_t = A("k_t", [P, NT, 3 * P])
    sp_t = A("sp_t", [P, NC, 4 * P])
    ssg = h_t[:, 0:2, :].rearrange("p a (b v) -> p (a b) v", v=DVG)
    ssh = h_t[:, 2:4, :].rearrange("p a (b h v) -> p (a b) h v", h=2, v=P)
    Gt = A("Gt", [P, 4, T])
    E2 = A("E2", [P, 2, T])
    glr = A("glr", [GR, T])
    wlr4 = A("wlr4", [GR, GH * P])
    wlr = A("wlr", [GR, P])
    blr4 = A("blr4", [P, GH])
    blr = A("blr", [P, 1])
    ones = A("ones", [P, P])
    mask = A("mask", [P, NL, C // 2])
    rowm = A("rowm", [TS, NB])
    tick = A("tick", [1, 1])
    pool_w = A("pool_w", [1, 2])
    onm = A("onm", [P, 3])
    lb = A("lb", [P, 6, HH])
    lbj = A("lbj", [P, 2, 2])
    dec = A("dec", [P, 3, NC + NB])
    k_flat = k_t[:, :, :].rearrange("p a b -> p (a b)")
    kblk = [t[:, :, :].rearrange("p a b -> p (a b)")[0:TS, 0:NB * P].rearrange("p (b d) -> p b d", b=NB)
            for t in (T3, B, T3)]
    over, at = {1: Z[:, :, :]}, 0
    for L in (2, 4, 8, 16, 32, 64, 128):
        blocks = (T if L <= SL else TP) // L
        over[L] = B[:, :, :].rearrange("p a b -> p (a b)")[:, at:at + 3 * blocks].rearrange("p (h n) -> p h n", h=3)
        at += 3 * blocks
    assert at <= 3 * T
    xt = [h_t[:, c, :] for c in range(NT)]
    square = v_t[:, :, :].rearrange("p a b -> p (a b)")[:, 0:D]
    sqo = [Z[:, 0, :], Z[:, 1, :], Z[:, 2, :], T3[:, 2, :]]
    head_of = (0, 0, 1, 2)

    def second(ap, L):
        return ap.rearrange("p (n b) -> p n b", b=2 * L)[:, :, L:2 * L]

    block = nc.Block()
    with block:
        @block.sync
        def _(sp):
            for c in range(NT):
                sp.dma_start(xt[c][0:tok(c), :], xp_v[c] if c < NC else xs_v).then_inc(x_in[c], 16)
            load_unit(sp, 0, win_v[:, :, GLR:GLR + P])
            for t, v in ((gain[:, 0, :], norm_mix_pre), (gain[:, 1, :], hgrn_lb),
                         (onm[:, 0:2], gla_onorm), (onm[:, 2:3], hgrn_onorm), (blr4[:, :], gla_b_lr), (wlr4[:, :], gla_w_lr2.rearrange("o r d -> (o r) d"))):
                sp.dma_start(t, v).then_inc(small, 16)
            with nc.sync.Fori(0, G) as j:
                j18 = sp.snap(j * NU)
                for n, (col, width, t) in enumerate(UNITS):
                    first = (j * (width // P) + (col // P + t)) * P + col % P
                    sp.wait_ge(w_lo, j18 + (n + 1))
                    load_unit(sp, n + 1, win_v[:, :, bass.ds(first, P)])
            for u in range(UB, UB + 2):
                sp.wait_ge(w_lo, u)
                load_unit(sp, u, wout_v[:, :, (u - UB) * P:(u - UB + 1) * P])
            sp.wait_ge(w_lo, UB + 2)

        @block.gpsimd
        def _(pool):
            n = 0

            def hold(s, value):
                pool.wait_ge(s, value)
                nc.gpsimd.tensor_tensor(pool_w[:, 1:2], pool_w[:, 0:1], pool_w[:, 0:1], ALU.add)
                pool.drain()
            for t in (ident, ones, mask, rowm, pool_w):
                ins = nc.gpsimd.memset(t[:], 0.0 if t is ident else 1.0)
                ins.then_inc(consts, 1)
                n += 1
            pool.wait_ge(consts, n)
            nc.gpsimd.affine_select(out=ident[:], in_=ident[:], compare_op=ALU.not_equal, fill=1.0, base=0,
                                    pattern=[[-1, P]], channel_multiplier=1).then_inc(consts, 1)
            n += 1
            for i, L in enumerate(LEVELS):
                m = mask[:, i, :].rearrange("p (a r) -> p a r", r=L)
                nc.gpsimd.affine_select(out=m, in_=m, compare_op=ALU.is_ge, fill=0.0, base=0,
                                        pattern=[[-2 * L, C // 2 // L], [0, L]], channel_multiplier=1).then_inc(consts, 1)
                n += 1
                pool.wait_ge(consts, n)
                nc.gpsimd.affine_select(out=m, in_=m, compare_op=ALU.is_ge, fill=0.0, base=L - 1,
                                        pattern=[[2 * L, C // 2 // L], [0, L]], channel_multiplier=-1).then_inc(consts, 1)
                n += 1
            nc.gpsimd.affine_select(out=rowm[:], in_=rowm[:], compare_op=ALU.is_ge, fill=0.0, base=0,
                                    pattern=[[-SL, NB]], channel_multiplier=1).then_inc(consts, 1)
            n += 1
            pool.wait_ge(consts, n)
            nc.gpsimd.affine_select(out=rowm[:], in_=rowm[:], compare_op=ALU.is_ge, fill=0.0, base=SL - 1,
                                    pattern=[[SL, NB]], channel_multiplier=-1).then_inc(consts, 1)
            n += 1
            assert n == CONSTS, n
            pool.wait_ge(turned, KT)


            def load_states(j):
                pool.dma_start(ssg[:, :, :], head(gla_v(state_gla), j)).then_inc(st_in, 16)
                for i in range(2):
                    pool.dma_start(ssh[:, :, i, :], head(hgrn_v(state_hgrn), 2 * j + i)).then_inc(st_in, 16)

            def store_states(j, heads=2):
                hold(sp_s, j * 2 + 2)
                pool.dma_start(gla_prompt.rearrange("o b h k v -> k (o b h) v")[:, bass.ds(j, 1), :],
                               sp_t[:, NC - 1:NC, 0:DVG]).then_inc(st_out, 16)
                pool.dma_start(hgrn_prompt.rearrange("o b h k v -> k (o b h) v")[:, bass.ds(2 * j, 2), :],
                               sp_t[:, NC - 1, DVG:2 * DVG].rearrange("k (h v) -> k h v", h=2)).then_inc(st_out, 16)
                hold(ss_s, j * 4 + 2)
                pool.dma_start(head(gla_v(gla_sample), j), ssg[:, :, :]).then_inc(st_out, 16)
                for i in range(heads):
                    hold(ss_s, j * 4 + (3 + i))
                    pool.dma_start(head(hgrn_v(hgrn_sample), 2 * j + i), ssh[:, :, i, :]).then_inc(st_out, 16)

            load_states(0)
            with nc.gpsimd.Fori(0, G - 1) as j:
                store_states(j)
                hold(st_out, j * 80 + 80)
                load_states(j + 1)
            store_states(G - 1, 1)

        @block.scalar
        def _(act):
            scratch = act.alloc_register("act_scratch")
            act.reg_mov(scratch, 0)
            act.preload_act_table_set("natural_log_exp_and_others")
            act.wait_ge(setup, SETUP)
            for c in range(NT):
                act.wait_ge(x_in[c], 16)
                act.activation(square[0:tok(c), :], xt[c][0:tok(c), :], ACT.Square, accum_out=stat[0:tok(c), 0, c:c + 1])
                act.drain()
            act.activation(stat[:, 1, :], stat[:, 0, :], ACT.Ln, scale=1.0 / D, bias=eps_c[:, :])
            act.drain()
            act.activation(stat[:, 1, :], stat[:, 1, :], ACT.Exp, scale=-0.5).then_inc(squared, 1)
            for u in range(2):
                act.wait_ge(w_raw[u % NRAW], loaded(u))
                split_hi(u)
            for k in range(KT):
                if k == 0:
                    act.wait_ge(small, 16 * 6)
                act.wait_ge(turned, k + 1)
                act.activation(x_hi[:, k, :], turn_slot(ps, k)[:, 0:T], ACT.Copy, scale=gain[:, 0, k:k + 1]).then_inc(x_hi_s, 1)
            act.wait_ge(w_raw[2 % NRAW], loaded(2))
            split_hi(2)
            act.wait_ge(lb_d, 1)
            act.activation(lb[:, 1, :], lb[:, 1, :], ACT.Exp).then_inc(lb_a, 1)
            act.wait_ge(lb_d, 2)
            act.activation(lb[:, 5, :], lb[:, 5, :], ACT.Ln, scale=-1.0, bias=one_c[:, :]).then_inc(lb_a, 1)
            act.wait_ge(unit_done, 1)
            act.activation(halves(glr[:, :]), proj(0)[0:GR], ACT.Copy).then_inc(unit_free, 1)
            with nc.scalar.Fori(0, G) as j:
                j18 = act.snap(j * NU)
                jr = act.snap(j * NR)
                hold = lambda s, v: held(act, scratch, s, v)

                def step(name):
                    hold(step_done, jr + (STEP[name] + 1))

                def freed(ins, name):
                    ins.then_inc(step_free[STEP[name] % 2], 1)

                def evacuate(n):
                    hold(unit_done, j18 + (n + 2))
                    src = proj(n + 1)
                    if n < 2:
                        if n == 0:
                            hold(merged_s, j + 1)
                        act.activation(halves(Z[:, 1 + n, :]), src, ACT.Copy).then_inc(unit_free, 1)
                    elif n == 2:
                        act.activation(halves(K[:, 0, :]), src, ACT.Copy).then_inc(unit_free, 1)
                    elif n < 6:
                        act.activation(halves(Q[:, n - 3, :]), src, ACT.Copy,
                                       scale=float(P) ** -0.5 if n == 3 else 1.0).then_inc(unit_free, 1)
                    elif n < GATE0:
                        act.activation(halves(Gt[:, n - 6, :]), src, ACT.Copy).then_inc(unit_free, 1)
                    elif n % 2 == 0:
                        hold(gate_s, j * 4 + ((n - GATE0) // 2 + 1))
                        act.activation(halves(E2[:, 0, :]), src, ACT.Sigmoid).then_inc(unit_free, 1)
                    else:
                        act.activation(halves(E2[:, 1, :]), src, ACT.Sigmoid)
                        act.activation(halves(Gt[:, (n - GATE0) // 2, :]), src, ACT.Copy).then_inc(unit_free, 1)

                def spread(h):
                    for b in range(NB):
                        ins = act.activation(kblk[h][:, b, :], k_t[0:TS, NC, h * P:(h + 1) * P], ACT.Copy, scale=rowm[:, b:b + 1])
                    ins.then_inc(kblk_s, 1)

                def output(d):
                    step(f"o{d}")
                    act.activation(L4[:, d, :], slot(STEP[f"o{d}"])[:, 0:T], ACT.Copy)
                    freed(act.activation(sqo[d], slot(STEP[f"o{d}"])[:, 0:T], ACT.Square), f"o{d}")
                    act.drain().then_inc(o_sq, 1)

                def turn_v(d):
                    step(f"v{d}")
                    s = slot(STEP[f"v{d}"])
                    act.activation(v_t[:, 0:NC, d * P:(d + 1) * P], s[:, 0:TP].rearrange("p (c v) -> p c v", c=NC), ACT.Copy)
                    ins = act.activation(v_t[0:TS, NC, d * P:(d + 1) * P], s[0:TS, TP:TP + P], ACT.Copy)
                    freed(ins, f"v{d}")

                act.preload_act_table_set("natural_log_exp_and_others")
                for n in range(NU):
                    if n == 10:
                        act.preload_act_table_set("sigmoid_and_others")
                    hold(w_raw[(n + 3) % NRAW], loaded(n + 3, j * (NU // NRAW)))
                    hold(unit_done, j18 + (n + 1))
                    split_hi(n + 3)
                    if n >= 1:
                        evacuate(n - 1)
                    if n == 2:
                        hold(lbj_s, j * 4 + 4)
                        step("decay")
                        freed(act.activation(halves(Z[:, 0, :]), slot(STEP["decay"]).rearrange("p (a b) -> p a b", a=2)[:, :, 0:HT],
                                             ACT.Identity, bias=blr[:, :]), "decay")
                        act.drain()
                        act.activation(T3[:, :, :], Z[:, :, :], ACT.Abs)
                        act.drain()
                        act.activation(T3[:, :, :], T3[:, :, :], ACT.Exp, scale=-1.0)
                        act.drain()
                        act.activation(T3[:, :, :], T3[:, :, :], ACT.Ln, bias=one_c[:, :]).then_inc(z_abs, 1)
                    if n == 4:
                        hold(l_dve, j + 1)
                        act.activation(Z[:, 0, :], L4[:, 0, :], ACT.Exp, scale=1.0 / TAU)
                        for h in range(2):
                            act.activation(Z[:, 1 + h, :], L4[:, 1 + h, :], ACT.Exp, bias=lbj[:, 0, h:h + 1])
                            act.activation(K[:, 1 + h, :], K[:, 1 + h, :], ACT.Exp, bias=lbj[:, 0, h:h + 1])
                        act.drain().then_inc(l2_act, 1)
                    if n == 6:
                        act.drain().then_inc(qk_in, 1)
                    if 8 <= n < 12:
                        turn_v(n - 8)
                    if 7 <= n <= 10:
                        act.drain().then_inc(v_in, 1)
                    if n > GATE0 and (n - GATE0) % 2 == 0:
                        act.drain().then_inc(gate_in, 1)
                    if n == 15:
                        step("kt0")
                        freed(act.activation(k_flat[:, 0:8 * P], slot(STEP["kt0"]), ACT.Copy), "kt0")
                        step("kt1")
                        act.activation(k_flat[:, 8 * P:12 * P], slot(STEP["kt1"])[:, 0:4 * P], ACT.Copy)
                        freed(act.activation(k_flat[0:TS, 12 * P:15 * P], slot(STEP["kt1"])[0:TS, 4 * P:7 * P], ACT.Copy), "kt1")
                        act.drain().then_inc(k_tok, 1)
                        spread(0)
                    if n == 16:
                        hold(dec_s, j + 1)
                        spread(1)
                    if n == 17:
                        for d in range(3):
                            output(d)
                        step("ss1")
                        spread(2)
                evacuate(NU - 1)
                act.drain().then_inc(gate_in, 1)
                act.preload_act_table_set("natural_log_exp_and_others")
                output(3)
                for h in range(3):
                    step(f"norm{h}")
                    freed(act.activation(Z[:, h, :], slot(STEP[f"norm{h}"])[:, 0:T], ACT.Ln,
                                         scale=1.0 / (DVG if h == 0 else P), bias=eps_c[:, :]), f"norm{h}")
                    act.drain()
                    act.activation(Z[:, h, :], Z[:, h, :], ACT.Exp, scale=-0.5).then_inc(rst, 1)
            act.wait_ge(unit_done, UB)
            act.wait_ge(merged_s, G)
            for k in range(KT - 2):
                act.activation(x_hi[:, k, :], merged[:, k, :], ACT.Copy).then_inc(m_hi, 1)

        @block.vector
        def _(dve):
            dve.memset(eps_c[:, :], EPS)
            dve.memset(one_c[:, :], 1.0)
            dve.memset(stat[:, :, :], 1.0).then_inc(setup, 1)
            dve.drain().then_inc(w_lo, 1)
            dve.drain().then_inc(unit_free, 1)
            dve.drain().then_inc(step_free[0], 1)
            dve.drain().then_inc(step_free[1], 1)
            dve.drain().then_inc(gate_s, 1)
            dve.drain().then_inc(merged_s, 1)
            dve.wait_ge(squared, 1)
            for c in range(NT):
                dve.tensor_scalar(xt[c][0:tok(c), :], xt[c][0:tok(c), :], stat[0:tok(c), 1, c:c + 1], None, ALU.mult).then_inc(scaled, 1)
            dve.wait_ge(small, 16 * 6)
            for k in range(KT):
                dve.wait_ge(x_hi_s, k + 1)
                dve.scalar_tensor_tensor(x_lo[:, k, :], turn_slot(ps, k)[:, 0:T], gain[:, 0, k:k + 1],
                                         x_hi[:, k, :].bitcast(F32), ALU.mult, ALU.subtract).then_inc(x_lo_s, 1)
                if k in (KT - 4, KT - 1):
                    u = (KT - 4, KT - 1).index(k)
                    dve.wait_ge(w_hi, u + 1)
                    split_lo(u)
            dve.wait_ge(w_hi, 3)
            split_lo(2)
            dve.tensor_tensor(lb[:, 1, :], gain[:, 1, :], gain[:, 1, :], ALU.subtract).then_inc(lb_d, 1)
            dve.wait_ge(lb_a, 1)
            dve.reciprocal(lb[:, 2, :], lb[:, 1, :])
            dve.drain()
            dve.tensor_tensor(lb[:, 1, :], lb[:, 1, :], lb[:, 2, :], ALU.mult)
            dve.drain()
            dve.tensor_tensor(lb[:, 3, :], lb[:, 1, :], lb[:, 1, :], ALU.subtract)
            dve.drain()
            dve.tensor_scalar(lb[:, 5, :], lb[:, 3, :], 0.0, 1.0 - 1e-6, ALU.max, ALU.min)
            dve.drain()
            dve.tensor_scalar(lb[:, 4, :], lb[:, 5, :], 1e-20, None, ALU.max).then_inc(lb_d, 1)
            dve.wait_ge(lb_a, 2)
            dve.wait_ge(consts, CONSTS)
            with nc.vector.Fori(0, G) as j:
                j18 = dve.snap(j * NU)
                jr = dve.snap(j * NR)

                def step(name):
                    dve.wait_ge(step_done, jr + (STEP[name] + 1))

                def freed(ins, name):
                    ins.then_inc(step_free[STEP[name] % 2], 1)

                def blocks_of(t, L):
                    if L > SL:
                        return t[:, :, 0:TP].rearrange("p h (n b) -> p h n b", b=L)
                    return t[:, :, :].rearrange("p h (n b) -> p (h n) b", b=L)

                def block_decays():
                    for L in LEVELS:
                        n = over[2 * L].shape[2]
                        two = over[L][:, :, 0:2 * n].rearrange("p h (n b) -> p h n b", b=2)
                        dve.tensor_tensor(over[2 * L].rearrange("p h (n o) -> p h n o", o=1), two[:, :, :, 0:1], two[:, :, :, 1:2], ALU.mult)
                        dve.drain()
                    dve.tensor_copy(dec[:, :, 0:NC], over[C])
                    dve.tensor_copy(dec[:, :, NC:NC + NB], over[SL][:, :, TP // SL:T // SL]).then_inc(dec_s, 1)

                def level_next(i):
                    step(f"level{i}")
                    L = LEVELS[i]
                    q, k = blocks_of(Q, 2 * L), blocks_of(K, 2 * L)
                    if 2 * L > SL:
                        n = TP // (2 * L)
                        two = over[L][:, :, 0:2 * n].rearrange("p h (n b) -> p h n b", b=2)
                        shape = [P, 3, n, L]
                        kf, qf = k[:, :, :, 0:L], q[:, :, :, L:2 * L]
                        first, behind = two[:, :, :, 0:1], two[:, :, :, 1:2]
                    else:
                        two = over[L].rearrange("p h (n b) -> p (h n) b", b=2)
                        shape = [P, 3 * T // (2 * L), L]
                        kf, qf = k[:, :, 0:L], q[:, :, L:2 * L]
                        first, behind = two[:, :, 0:1], two[:, :, 1:2]
                    dve.tensor_tensor(qf, qf, first.broadcast_to(shape), ALU.mult)
                    ins = dve.tensor_tensor(kf, kf, behind.broadcast_to(shape), ALU.mult)
                    ins.then_inc(lvl if i < NL - 1 else qs, 1)

                def level_take(i):
                    dve.drain()
                    step(f"level{i}")
                    dve.memset(tick[:, :], 0.0)
                    L = LEVELS[i]
                    s = slot(STEP[f"level{i}"])
                    n = C // 2 // L
                    m = mask[:, i, :].bitcast(I32).rearrange("p (o a r) -> p o a r", o=1, r=L)
                    ins = dve.copy_predicated(
                        Am[:, :, :].rearrange("p h (a b) -> p h a b", b=2 * L)[:, :, :, L:2 * L],
                        m.broadcast_to([P, 3 * NC, n, L]),
                        s[:, 0:3 * NC * C // 2].rearrange("p (h a r) -> p h a r", a=n, r=L))
                    if L <= 4:
                        n = TS // 2 // L
                        o = 3 * NC * C // 2
                        ins = dve.copy_predicated(
                            As[:, :, :].rearrange("p h (a b) -> p h a b", b=2 * L)[:, :, :, L:2 * L],
                            m[0:TS, :, 0:n, :].broadcast_to([TS, 3, n, L]),
                            s[0:TS, o:o + 3 * TS // 2].rearrange("p (h a r) -> p h a r", a=n, r=L))
                    freed(ins, f"level{i}")

                def diagonal(i):
                    step(f"diag{i}")
                    s = slot(STEP[f"diag{i}"])
                    if i < 2:
                        ins = dve.tensor_tensor(Am[:, 6 * i:6 * i + 6, :], s[:, 0:6 * C].rearrange("p (h t) -> p h t", t=C),
                                                ident[:, :].rearrange("p (o t) -> p o t", o=1).broadcast_to([P, 6, C]), ALU.mult)
                    else:
                        ins = dve.tensor_tensor(As[:, :, :], s[0:TS, 0:3 * TS].rearrange("p (h t) -> p h t", t=TS),
                                                ident[0:TS, 0:TS].rearrange("p (o t) -> p o t", o=1).broadcast_to([TS, 3, TS]), ALU.mult)
                    freed(ins, f"diag{i}")

                def gate(t):
                    dve.wait_ge(gate_in, j * 4 + (t + 1))
                    dve.tensor_tensor(E2[:, 0, :], E2[:, 0, :], E2[:, 1, :], ALU.mult)
                    dve.drain()
                    dve.scalar_tensor_tensor(Gt[:, t, :], Gt[:, t, :], onm[:, min(t, 2):min(t, 2) + 1], E2[:, 0, :],
                                             ALU.mult, ALU.mult).then_inc(gate_s, 1)

                dve.tensor_copy(wlr[:, :], wlr4[:, bass.ds(j * P, P)]).then_inc(lbj_s, 1)
                dve.tensor_copy(blr[:, :], blr4[:, bass.ds(j, 1)]).then_inc(lbj_s, 1)
                for a, b in ((0, 5), (1, 4)):
                    dve.tensor_copy(lbj[:, a, :], lb[:, b, bass.ds(2 * j, 2)]).then_inc(lbj_s, 1)
                dve.drain()
                for n in range(NU):
                    if 8 <= n < 8 + NL:
                        level_next(n - 8)
                    dve.wait_ge(w_hi, j18 + (n + 4))
                    split_lo(n + 3)
                    if n == 3:
                        dve.wait_ge(z_abs, j + 1)
                        dve.scalar_tensor_tensor(L4[:, 0:3, :], Z[:, :, :], 0.0, T3[:, :, :], ALU.min, ALU.subtract)
                        dve.drain()
                        dve.tensor_tensor(K[:, 1:3, :], L4[:, 1:3, :], Z[:, 1:3, :], ALU.subtract).then_inc(l_dve, 1)
                    if n == 5:
                        dve.wait_ge(l2_act, j + 1)
                        for h in range(2):
                            dve.tensor_scalar(Z[:, 1 + h, :], Z[:, 1 + h, :], lbj[:, 1, h:h + 1], None, ALU.add)
                        dve.drain()
                        block_decays()
                    if n == 7:
                        diagonal(0)
                        diagonal(1)
                        diagonal(2)
                        dve.tensor_tensor(Q[:, :, :], Q[:, :, :], Z[:, :, :], ALU.mult).then_inc(lvl, 1)
                    if 8 <= n < 8 + NL:
                        level_take(n - 8)
                    if n == 7 + NL:
                        dve.drain().then_inc(a_s, 1)
                    if n > GATE0 and (n - GATE0) % 2 == 0:
                        gate((n - GATE0) // 2 - 1)
                    if n == 16:
                        dve.wait_ge(st_in, j * 48 + 48)
                        dve.memset(tick[:, :], 0.0)
                        for i in range(2):
                            dve.drain()
                            step(f"ds{i}")
                            s = slot(STEP[f"ds{i}"])
                            for c in (2 * i, 2 * i + 1):
                                dS = s[:, (c % 2) * 4 * P:(c % 2 + 1) * 4 * P]
                                if c == 0:
                                    ins = dve.tensor_copy(sp_t[:, 0, :], dS)
                                else:
                                    if c != 2:
                                        dve.drain()
                                    for h, (a, b) in enumerate(((0, 256), (256, 384), (384, 512))):
                                        ins = dve.scalar_tensor_tensor(sp_t[:, c, a:b], sp_t[:, c - 1, a:b], dec[:, h, c:c + 1],
                                                                       dS[:, a:b], ALU.mult, ALU.add)
                            freed(ins, f"ds{i}")
                            dve.drain().then_inc(sp_s, 1)
                def sample_states(i):
                    step(f"ss{i}")
                    h = (0, 0, 1, 2)[i]
                    w = DVG if h == 0 else P
                    for b in (range(4 * i, 4 * i + 4) if i < 2 else range(NB)):
                        st = ssg[:, b, :] if h == 0 else ssh[:, b, h - 1, :]
                        ins = dve.scalar_tensor_tensor(st, st, dec[:, h, NC + b:NC + b + 1],
                                                       slot(STEP[f"ss{i}"])[:, (b * w) % 1024:(b * w) % 1024 + w], ALU.mult, ALU.add)
                    freed(ins, f"ss{i}")
                    dve.drain().then_inc(ss_s, 1)

                for i in range(3):
                    sample_states(i)
                gate(3)
                dve.drain()
                for d in range(4):
                    dve.wait_ge(o_sq, j * 4 + (d + 1))
                    dve.tensor_tensor(L4[:, d, :], L4[:, d, :], Gt[:, d, :], ALU.mult)
                dve.drain()
                dve.wait_ge(rst, j * 3 + 1)
                dve.tensor_tensor(L4[:, 0:2, :], L4[:, 0:2, :], Z[:, 0:1, :].broadcast_to([P, 2, T]), ALU.mult)
                dve.wait_ge(rst, j * 3 + 3)
                dve.tensor_tensor(L4[:, 2:4, :], L4[:, 2:4, :], Z[:, 1:3, :], ALU.mult)
                dve.drain()
                dve.tensor_tensor(merged[:, bass.ds(2 * j, 2), :], L4[:, 0:2, :], L4[:, 2:4, :], ALU.add).then_inc(merged_s, 1)
                sample_states(3)

        @block.tensor
        def _(pe):
            pe.wait_ge(consts, CONSTS)
            for k in range(KT):
                if k >= 4:
                    pe.wait_ge(x_lo_s, k - 3)
                for c in range(NT):
                    if k == 0:
                        pe.wait_ge(scaled, c + 1)
                    m = nc.tensor.transpose(turn_slot(ps, k)[:, c * P:c * P + tok(c)], xt[c][0:tok(c), k * P:(k + 1) * P],
                                            ident[0:tok(c), 0:tok(c)])
                m.then_inc(turned, 1)
            pe.wait_ge(w_lo, 2)
            pe.wait_ge(x_lo_s, KT - 3)
            unit_passes(0, proj(0), xh, xl, ready=lambda k: pe.wait_ge(x_lo_s, k + 1)).then_inc(unit_done, 1)
            with nc.tensor.Fori(0, G) as j:
                j18 = pe.snap(j * NU)
                jh = pe.snap(j * (NR // 2))

                def taken(name):
                    pe.wait_ge(step_free[STEP[name] % 2], jh + (STEP[name] // 2 + 1))

                def do_step(name):
                    r = STEP[name]
                    s = slot(r)
                    taken(name)
                    if name == "decay":
                        pe.wait_ge(lbj_s, j * 4 + 4)
                        for q in range(2):
                            m = nc.tensor.matmul(s[:, q * 512:q * 512 + HT], wlr[:, :], glr[:, q * HT:(q + 1) * HT], start=True, stop=True)
                    elif name[0] == "v":
                        d = int(name[1:])
                        pe.wait_ge(v_in, j * 4 + (d + 1))
                        for c in range(NT):
                            m = nc.tensor.transpose(s[0:tok(c), c * P:(c + 1) * P], Gt[:, d, c * P:c * P + tok(c)], ident[:, :])
                    elif name[:4] == "diag":
                        i = int(name[4:])
                        if i == 0:
                            pe.wait_ge(qk_in, j + 1)
                        for a in range(6 if i < 2 else 0):
                            c, h = divmod(6 * i + a, 3)
                            m = nc.tensor.matmul(s[:, a * C:(a + 1) * C], K[:, h, c * C:(c + 1) * C], Q[:, h, c * C:(c + 1) * C],
                                                 start=True, stop=True)
                        if i == 2:
                            for h in range(3):
                                m = nc.tensor.matmul(s[0:TS, h * TS:(h + 1) * TS], K[:, h, TP:T], Q[:, h, TP:T],
                                                     start=True, stop=True)
                    elif name[:5] == "level":
                        i = int(name[5:])
                        L = LEVELS[i]
                        pe.wait_ge(lvl, j * NL + (i + 1))
                        for a in range(3 * NC):
                            c, h = divmod(a, 3)
                            m = nc.tensor.matmul(s[:, a * C // 2:(a + 1) * C // 2], K[:, h, c * C:(c + 1) * C], second(Q[:, h, c * C:(c + 1) * C], L),
                                                 start=True, stop=True)
                        if L <= 4:
                            for h in range(3):
                                o = 3 * NC * C // 2 + h * TS // 2
                                m = nc.tensor.matmul(s[0:TS, o:o + TS // 2], K[:, h, TP:T], second(Q[:, h, TP:T], L), start=True, stop=True)
                    elif name[:2] == "kt":
                        i = int(name[2:])
                        if i == 0:
                            pe.wait_ge(qs, j + 1)
                        for a in (range(8) if i == 0 else range(8, 3 * NT)):
                            c, h = divmod(a, 3)
                            m = nc.tensor.transpose(s[0:tok(c), (a % 8) * P:(a % 8 + 1) * P], K[:, h, c * P:c * P + tok(c)], ident[:, :])
                    elif name[:2] == "ds":
                        i = int(name[2:])
                        pe.wait_ge(k_tok, j + 1)
                        for c in (2 * i, 2 * i + 1):
                            for h, (a, b) in enumerate(((0, 256), (256, 384), (384, 512))):
                                o = (c % 2) * 512
                                m = nc.tensor.matmul(s[:, o + a:o + b], k_t[:, c, h * P:(h + 1) * P], v_t[:, c, a:b], start=True, stop=True)
                    elif name[0] == "o":
                        d = int(name[1:])
                        h = head_of[d]
                        cols = slice(d * P, (d + 1) * P)
                        if d == 0:
                            pe.wait_ge(a_s, j + 1)
                            pe.wait_ge(sp_s, j * 2 + 2)
                            pe.wait_ge(st_in, j * 48 + 48)
                        for c in range(NC):
                            m = nc.tensor.matmul(s[:, c * C:(c + 1) * C], v_t[:, c, cols], Am[:, 3 * c + h, :], start=True, stop=(c == 0))
                            if c > 0:
                                m = nc.tensor.matmul(s[:, c * C:(c + 1) * C], sp_t[:, c - 1, cols], Q[:, h, c * C:(c + 1) * C],
                                                     start=False, stop=True)
                        for b in range(NB):
                            st = ssg[:, b, cols] if d < 2 else ssh[:, b, d - 2, :]
                            nc.tensor.matmul(s[:, TP + b * SL:TP + (b + 1) * SL], st, Q[:, h, TP + b * SL:TP + (b + 1) * SL],
                                             start=(b == 0), stop=False, skip_group_check=True)
                        m = nc.tensor.matmul(s[:, TP:T], v_t[0:TS, NC, cols], As[:, h, :], start=False, stop=True, skip_group_check=True)
                    elif name[:4] == "norm":
                        h = int(name[4:])
                        pe.wait_ge(o_sq, j * 4 + (2, 3, 4)[h])
                        for a, b in ((0, TP), (TP, T)):
                            for d in ((0, 1), (2,), (3,))[h]:
                                m = nc.tensor.matmul(s[:, a:b], ones[:, :], sqo[d][:, a:b], start=(d in (0, 2, 3)), stop=(d in (1, 2, 3)))
                    elif name[:2] == "ss":
                        i = int(name[2:])
                        pe.wait_ge(kblk_s, j * 3 + (1, 1, 2, 3)[i])
                        for b in (range(4 * i, 4 * i + 4) if i < 2 else range(NB)):
                            if i < 2:
                                o, v = (b % 4) * DVG, v_t[0:TS, NC, 0:DVG]
                            else:
                                o, v = b * P, v_t[0:TS, NC, i * P:(i + 1) * P]
                            m = nc.tensor.matmul(s[:, o:o + v.shape[-1]], kblk[(0, 0, 1, 2)[i]][:, b, :], v, start=True, stop=True)
                    m.then_inc(step_done, 1)

                for n in range(NU):
                    pe.wait_ge(unit_free, j18 + (n + 1))
                    pe.wait_ge(w_lo, j18 + (n + 3))
                    unit_passes(n + 1, proj(n + 1), xh, xl).then_inc(unit_done, 1)
                    for name in AFTER.get(n, []):
                        do_step(name)
    sa.close()

    sbk = ExitStack()
    g_post = sb("g_post", [P, D], F32, sbk)
    mt = sb("mt", [P, KT, T], F32, sbk)
    g_pre = sb("g_pre", [P, D], F32, sbk)
    hn = sb("hn", [P, 3, D], F32, sbk)
    msq = sb("msq", [P, D], F32, sbk)
    last_head = h_t[:, 2:4, :].rearrange("p a (b h v) -> p (a b) h v", h=2, v=P)[:, :, 1, :]
    st_last = sem("st_last")
    h_in = sem("h_in")
    m_lo = sem("m_lo")
    m_tok = sem("m_tok")
    m_rms = sem("m_rms")
    m_half = sem("m_half")
    h_s = sem("h_s")
    h_rms = sem("h_rms")
    hn_s = sem("hn_s")
    h_turn = sem("h_turn")
    f_hi = sem("f_hi")
    f_lo = sem("f_lo")

    def turned_tile(c):
        return tok_slot(ps, c).rearrange("p (k t) -> p k t", k=KT)[:, :, 0:tok(c)]

    with nc.Block() as block:
        @block.sync
        def _(sp):
            sp.dma_start(head(hgrn_v(hgrn_sample), HH - 1), last_head).then_inc(st_last, 16)
            for u in range(UB + 2, UC + 2):
                sp.wait_ge(w_lo, u)
                src = wout_v[:, :, (u - UB) * P:(u - UB + 1) * P] if u < UC else wf1_v[:, :, (u - UC) * FF:(u - UC) * FF + P]
                load_unit(sp, u, src)
                if u == UB + 4:
                    sp.wait_ge(st_out, 80 * G - 16)
                    sp.wait_ge(st_last, 16)
                    for c in range(NT):
                        sp.dma_start(h_t[0:tok(c), c, :], xp_v[c] if c < NC else xs_v).then_inc(h_in, 16)
                    sp.dma_start(g_post[:, :], norm_mix_post.partition_broadcast(P).rearrange("p o d -> p (o d)")).then_inc(h_in, 16)
                    sp.dma_start(g_pre[:, :], norm_ffn_pre.partition_broadcast(P).rearrange("p o d -> p (o d)")).then_inc(h_in, 16)

        @block.scalar
        def _(act):
            for k in range(KT - 2, KT):
                act.activation(x_hi[:, k, :], merged[:, k, :], ACT.Copy).then_inc(m_hi, 1)
            for u in range(UB, UC):
                act.wait_ge(w_raw[(u + 2) % NRAW], loaded(u + 2))
                act.wait_ge(unit_done, u)
                split_hi(u + 2)
                act.wait_ge(unit_done, u + 1)
                act.activation(halves(mt[:, u - UB, :]), proj(u), ACT.Copy).then_inc(unit_free, 1)
            def rms(c, src, done):
                n = tok(c)
                act.activation(msq[0:n, :], src, ACT.Square, accum_out=stat[0:n, 0, c:c + 1])
                act.drain()
                act.activation(stat[0:n, 1, c:c + 1], stat[0:n, 0, c:c + 1], ACT.Ln, scale=1.0 / D, bias=eps_c[0:n, :])
                act.drain()
                act.activation(stat[0:n, 1, c:c + 1], stat[0:n, 1, c:c + 1], ACT.Exp, scale=-0.5).then_inc(done, 1)

            for i in range(NT + 2):
                if i < NT:
                    act.wait_ge(m_tok, i + 1)
                    rms(i, tok_slot(ps, i)[0:tok(i), :], m_rms)
                if 1 <= i <= NT:
                    act.wait_ge(h_s, i)
                    rms(i - 1, h_t[0:tok(i - 1), i - 1, :], h_rms)
                if i >= 2:
                    c = i - 2
                    act.wait_ge(h_turn, c + 1)
                    act.activation(x_hi[:, :, c * P:c * P + tok(c)], turned_tile(c), ACT.Copy).then_inc(f_hi, 1)

        @block.vector
        def _(dve):
            for k in range(KT):
                dve.wait_ge(m_hi, k + 1)
                dve.tensor_tensor(x_lo[:, k, :], merged[:, k, :], x_hi[:, k, :].bitcast(F32), ALU.subtract).then_inc(m_lo, 1)
            for u in range(UB, UC):
                dve.wait_ge(w_hi, u + 3)
                split_lo(u + 2)
            dve.wait_ge(h_in, 16 * (NT + 2))
            for i in range(NT + 2):
                if i < NT:
                    n, half = tok(i), hn[0:tok(i), i % 3, :]
                    dve.wait_ge(m_rms, i + 1)
                    if i >= 3:
                        dve.wait_ge(h_turn, i - 2)
                    dve.scalar_tensor_tensor(half, tok_slot(ps, i)[0:n, :], stat[0:n, 1, i:i + 1], g_post[0:n, :],
                                             ALU.mult, ALU.mult).then_inc(m_half, 1)
                    dve.drain()
                    dve.tensor_tensor(h_t[0:n, i, :], h_t[0:n, i, :], half, ALU.add).then_inc(h_s, 1)
                if 1 <= i <= NT:
                    c = i - 1
                    n = tok(c)
                    dve.wait_ge(h_rms, c + 1)
                    dve.scalar_tensor_tensor(hn[0:n, c % 3, :], h_t[0:n, c, :], stat[0:n, 1, c:c + 1], g_pre[0:n, :],
                                             ALU.mult, ALU.mult).then_inc(hn_s, 1)
                if i >= 2:
                    c = i - 2
                    dve.wait_ge(f_hi, c + 1)
                    cols = slice(c * P, c * P + tok(c))
                    dve.tensor_tensor(x_lo[:, :, cols], turned_tile(c), x_hi[:, :, cols].bitcast(F32), ALU.subtract).then_inc(f_lo, 1)

        @block.tensor
        def _(pe):
            for u in range(UB, UC):
                pe.wait_ge(unit_free, u)
                pe.wait_ge(w_lo, u + 2)
                unit_passes(u, proj(u), xh, xl,
                            ready=(lambda k: pe.wait_ge(m_lo, k + 1)) if u == UB else None).then_inc(unit_done, 1)

            def turn_m(c):
                if c >= 4:
                    pe.wait_ge(f_lo, c - 3)
                for k in range(KT):
                    m = nc.tensor.transpose(tok_slot(ps, c)[0:tok(c), k * P:(k + 1) * P], mt[:, k, c * P:c * P + tok(c)], ident[:, :])
                m.then_inc(m_tok, 1)

            pe.wait_ge(unit_free, UC + 1)
            for c in range(4):
                turn_m(c)
            for c in range(NT):
                n = tok(c)
                if c == 2:
                    turn_m(4)
                pe.wait_ge(m_half, c + 1)
                pe.wait_ge(hn_s, c + 1)
                for k in range(KT):
                    m = nc.tensor.transpose(tok_slot(ps, c)[:, k * P:k * P + n], hn[0:n, c % 3, k * P:(k + 1) * P], ident[0:n, 0:n])
                m.then_inc(h_turn, 1)
    sbk.close()
    merged_stack.close()

    act_hi = sb("act_hi", [P, FT, T], F32R)
    act_lo = sb("act_lo", [P, FT, T], F32R)
    sc = ExitStack()
    fe = sb("fe", [P, 2, T], F32, sc)
    fa = sb("fa", [P, 2, T], F32, sc)
    hs_out = sem("hs_out")
    ff_a = sem("ff_a")
    ff_l = sem("ff_l")
    PAIRS = 3
    LOOPS = (FT - 1) // PAIRS
    with nc.Block() as block:
        @block.sync
        def _(sp):
            sp.dma_start(ys_v, h_t[0:TS, NC, :]).then_inc(hs_out, 16)
            with nc.sync.Fori(0, LOOPS) as i:
                i6 = sp.snap(i * 2 * PAIRS)
                for n in range(2 * PAIRS):
                    first = sp.snap(i * (PAIRS * P) + ((n // 2 + 1) * P + n % 2 * FF))
                    sp.wait_ge(w_lo, i6 + (UC + 2 + n))
                    load_unit(sp, UC + 2 + n, wf1_v[:, :, bass.ds(first, P)])
            for n in range(2):
                sp.wait_ge(w_lo, UD + n)
                load_unit(sp, UD + n, wf2_v[:, KCUT[n][0]:KCUT[n][0] + KCUT[n][1], 0:P], KCUT[n][1])

        @block.scalar
        def _(act):
            scratch = act.alloc_register("act_scratch_c")
            act.reg_mov(scratch, 0)

            def pair(i6, i3, p):
                for n in (2 * p, 2 * p + 1):
                    held(act, scratch, w_raw[(UC + n + 2) % NRAW], loaded(UC + n + 2, i3))
                    held(act, scratch, unit_done, i6 + (UC + n))
                    split_hi(UC + n + 2, KT)
                    held(act, scratch, unit_done, i6 + (UC + n + 1))
                    if n % 2 == 0:
                        held(act, scratch, ff_l, i3 + (p + 1))
                        act.activation(halves(fe[:, 0, :]), proj(UC + n), ACT.Sigmoid)
                        act.activation(halves(fa[:, 0, :]), proj(UC + n), ACT.Copy).then_inc(unit_free, 1)
                        act.drain().then_inc(ff_a, 1)
            with nc.scalar.Fori(0, LOOPS) as i:
                i6 = act.snap(i * 2 * PAIRS)
                i3 = act.snap(i * PAIRS)
                act.preload_act_table_set("sigmoid_and_others")
                for p in range(PAIRS):
                    pair(i6, i3, p)
            pair(2 * PAIRS * LOOPS, PAIRS * LOOPS, 0)

        @block.vector
        def _(dve):
            dve.memset(fe[:, :, 0:1], 0.0).then_inc(ff_l, 1)

            def pair(i6, i3, p, row):
                for n in (2 * p, 2 * p + 1):
                    dve.wait_ge(w_hi, i6 + (UC + n + 3))
                    split_lo(UC + n + 2)
                dve.wait_ge(ff_a, i3 + (p + 1))
                dve.tensor_tensor(fa[:, 0, :], fa[:, 0, :], fe[:, 0, :], ALU.mult)
                dve.drain()
                dve.wait_ge(unit_done, i6 + (UC + 2 * p + 2))
                dve.tensor_tensor(halves(fe[:, 0, :]), halves(fa[:, 0, :]), proj(UC + 2 * p + 1), ALU.mult).then_inc(unit_free, 1)
                dve.drain()
                dve.tensor_copy(act_hi[:, row, :], fe[:, 0:1, :])
                dve.drain()
                dve.tensor_tensor(act_lo[:, row, :], fe[:, 0:1, :], act_hi[:, row, :].bitcast(F32), ALU.subtract).then_inc(ff_l, 1)
            with nc.vector.Fori(0, LOOPS) as i:
                i6 = dve.snap(i * 2 * PAIRS)
                i3 = dve.snap(i * PAIRS)
                for p in range(PAIRS):
                    pair(i6, i3, p, bass.ds(i * PAIRS + p, 1))
            pair(2 * PAIRS * LOOPS, PAIRS * LOOPS, 0, slice(FT - 1, FT))

        @block.tensor
        def _(pe):
            def pair(i6, p):
                for n in (2 * p, 2 * p + 1):
                    pe.wait_ge(unit_free, i6 + (UC + n))
                    pe.wait_ge(w_lo, i6 + (UC + n + 2))
                    unit_passes(UC + n, proj(UC + n), xh, xl).then_inc(unit_done, 1)
            with nc.tensor.Fori(0, LOOPS) as i:
                i6 = pe.snap(i * 2 * PAIRS)
                for p in range(PAIRS):
                    pair(i6, p)
            pair(2 * PAIRS * LOOPS, 0)
    sc.close()

    part = sb("part", [P, KT, NT])
    junk = x_lo[:, 0:NT, 0:P]
    f_t = sb("f_t", [P, T])
    f_main = sb("f_main", [P, NC, D])
    f_tok = [f_main[:, c, :] for c in range(NC)] + [h_t[:, NC, :]]
    h_back = w_raw_t[:, 0, :, :].rearrange("p k n -> p (k n)")
    h_tok = [h_t[:, c, :] for c in range(NC)] + [h_back]
    g_last = w_raw_t[:, 1, :, :].rearrange("p k n -> p (k n)")
    g_in = sem("g_in")
    h_back_s = sem("h_back_s")
    sq_s = sem("sq_s")
    sum_s = sem("sum_s")
    ft_s = sem("ft_s")
    ft_turn = sem("ft_turn")
    ft_tok = sem("ft_tok")
    y_rms = sem("y_rms")
    y_s = sem("y_s")
    y_out = sem("y_out")
    TILES = 2
    NCUT = len(KCUT)
    BODY = TILES * NCUT
    LOOPD = KT // TILES
    with nc.Block() as block:
        @block.sync
        def _(sp):
            def loads(i6, col, ns):
                for n in ns:
                    k0, nk = KCUT[n % NCUT]
                    where = col(n // NCUT)
                    sp.wait_ge(w_lo, i6 + (UD + n))
                    load_unit(sp, UD + n, wf2_v[:, k0:k0 + nk, where], nk)
            with nc.sync.Fori(0, LOOPD - 1) as i:
                i6 = sp.snap(i * BODY)
                loads(i6, lambda t: bass.ds(sp.snap(i * (TILES * P) + t * P), P), range(2, BODY + 2))
            i6 = (LOOPD - 1) * BODY
            loads(i6, lambda t: slice((LOOPD - 1) * TILES * P + t * P, (LOOPD - 1) * TILES * P + (t + 1) * P), range(2, BODY))
            sp.wait_ge(hs_out, 16)
            sp.wait_ge(w_lo, UD + KT * NCUT)
            sp.dma_start(g_last, norm_ffn_post.partition_broadcast(P).rearrange("p o d -> p (o d)")).then_inc(g_in, 16)
            sp.wait_ge(w_lo, UD + KT * NCUT + 1)
            sp.dma_start(h_back[0:TS, :], ys_v).then_inc(h_back_s, 16)
            sp.wait_ge(h_back_s, 16)
            for c in range(NT):
                sp.wait_ge(y_s, c + 1)
                sp.dma_start(yp_v[c] if c < NC else ys_v, f_tok[c][0:tok(c), :]).then_inc(y_out, 16)
            sp.wait_ge(y_out, 16 * NT)

        @block.gpsimd
        def _(pool):
            pool.wait_ge(st_out, 80 * G - 16)

        @block.scalar
        def _(act):
            scratch = act.alloc_register("act_scratch_d")
            act.reg_mov(scratch, 0)

            def body(i6, i3, i2, last, tile):
                for n in range(BODY):
                    if not last or n < BODY - 2:
                        held(act, scratch, w_raw[(UD + n + 2) % NRAW], loaded(UD + n + 2, i3))
                        held(act, scratch, unit_done, i6 + (UD + n))
                        split_hi(UD + n + 2, KCUT[(n + 2) % NCUT][1])
                    if n % NCUT == NCUT - 1:
                        m = n // NCUT
                        held(act, scratch, unit_done, i6 + (UD + n + 1))
                        held(act, scratch, ft_tok, i2 + (m + 2))
                        act.activation(halves(f_t[:, :]), proj(m), ACT.Copy).then_inc(ft_s, 1)
                    if n == NCUT + 1:
                        squares(i2, 0, tile)
                squares(i2, 1, tile)

            def squares(i2, m, tile):
                act.drain()
                held(act, scratch, ft_turn, i2 + (m + 1))
                for c in range(NT):
                    n = tok(c)
                    ins = act.activation(junk[0:n, c, :], slot(m)[0:n, c * P:(c + 1) * P], ACT.Square,
                                         accum_out=part[0:n, tile(m), c:c + 1])
                ins.then_inc(sq_s, 1)
            with nc.scalar.Fori(0, LOOPD - 1) as i:
                body(act.snap(i * BODY), act.snap(i * (BODY // NRAW)), act.snap(i * TILES), False, lambda m: bass.ds(i * TILES + m, 1))
            act.preload_act_table_set("natural_log_exp_and_others")
            body((LOOPD - 1) * BODY, (LOOPD - 1) * BODY // NRAW, (LOOPD - 1) * TILES, True,
                 lambda m: slice((LOOPD - 1) * TILES + m, (LOOPD - 1) * TILES + m + 1))
            act.wait_ge(sum_s, 1)
            act.activation(stat[:, 1, :], stat[:, 0, :], ACT.Ln, scale=1.0 / D, bias=eps_c[:, :])
            act.drain()
            act.activation(stat[:, 1, :], stat[:, 1, :], ACT.Exp, scale=-0.5).then_inc(y_rms, 1)

        @block.vector
        def _(dve):
            dve.memset(part[:, :, :], 0.0)
            for _ in range(2):
                dve.drain().then_inc(ft_tok, 1)

            def body(i6, i2, last, tile):
                for n in range(BODY):
                    if not last or n < BODY - 2:
                        dve.wait_ge(w_hi, i6 + (UD + n + 3))
                        split_lo(UD + n + 2, KCUT[(n + 2) % NCUT][1])
                    if n == NCUT + 1:
                        take(i2, 0, tile)
                if last:
                    dve.wait_ge(g_in, 16)
                    dve.drain()
                    done = D - P
                    dve.tensor_tensor(f_main[:, :, 0:done], f_main[:, :, 0:done],
                                      g_last[:, 0:done].rearrange("p (o v) -> p o v", o=1).broadcast_to([P, NC, done]), ALU.mult)
                    dve.tensor_tensor(f_tok[NC][0:TS, 0:done], f_tok[NC][0:TS, 0:done], g_last[0:TS, 0:done], ALU.mult)
                take(i2, 1, tile, last)

            dve.wait_ge(hs_out, 16)

            def take(i2, m, tile, gained=False):
                dve.wait_ge(sq_s, i2 + (m + 1))
                s = slot(m)
                if not gained:
                    dve.tensor_copy(f_main[:, :, tile(m)], s[:, 0:TP].rearrange("p (c v) -> p c v", c=NC))
                    dve.tensor_copy(f_tok[NC][0:TS, tile(m)], s[0:TS, TP:TP + P]).then_inc(ft_tok, 1)
                    return
                g = g_last[:, tile(m)]
                dve.tensor_tensor(f_main[:, :, tile(m)], s[:, 0:TP].rearrange("p (c v) -> p c v", c=NC),
                                  g.rearrange("p (o v) -> p o v", o=1).broadcast_to([P, NC, P]), ALU.mult)
                dve.tensor_tensor(f_tok[NC][0:TS, tile(m)], s[0:TS, TP:TP + P], g[0:TS], ALU.mult).then_inc(ft_tok, 1)
            with nc.vector.Fori(0, LOOPD - 1) as i:
                body(dve.snap(i * BODY), dve.snap(i * TILES), False, lambda m: bass.ds(i * (TILES * P) + m * P, P))
            base = (LOOPD - 1) * TILES * P
            body((LOOPD - 1) * BODY, (LOOPD - 1) * TILES, True, lambda m: slice(base + m * P, base + (m + 1) * P))
            dve.tensor_reduce(stat[:, 0, :], part[:, :, :].rearrange("p m c -> p c m"), mybir.AxisListType.X, ALU.add).then_inc(sum_s, 1)
            dve.wait_ge(h_back_s, 16)
            dve.wait_ge(y_rms, 1)
            for c in range(NT):
                n = tok(c)
                dve.scalar_tensor_tensor(f_tok[c][0:n, :], f_tok[c][0:n, :], stat[0:n, 1, c:c + 1], h_tok[c][0:n, :],
                                         ALU.mult, ALU.add).then_inc(y_s, 1)

        @block.tensor
        def _(pe):
            def turn(i2, m):
                pe.wait_ge(ft_s, i2 + (m + 1))
                for c in range(NT):
                    ins = nc.tensor.transpose(slot(m)[0:tok(c), c * P:(c + 1) * P], f_t[:, c * P:c * P + tok(c)], ident[:, :])
                ins.then_inc(ft_turn, 1)

            def body(i6, i2):
                for n in range(BODY):
                    m, cut = divmod(n, NCUT)
                    k0, nk = KCUT[cut]
                    pe.wait_ge(w_lo, i6 + (UD + n + 2))
                    if cut == 0:
                        pe.wait_ge(ft_tok, i2 + (m + 1))
                    unit_passes(UD + n, proj(m), lambda k, q: act_hi[:, k0 + k, q * HT:(q + 1) * HT],
                                lambda k, q: act_lo[:, k0 + k, q * HT:(q + 1) * HT], nk,
                                first=(cut == 0), last=(cut == NCUT - 1)).then_inc(unit_done, 1)
                    if m == 1 and cut == 0:
                        turn(i2, 0)
                turn(i2, 1)
            with nc.tensor.Fori(0, LOOPD - 1) as i:
                body(pe.snap(i * BODY), pe.snap(i * TILES))
            body((LOOPD - 1) * BODY, (LOOPD - 1) * TILES)
    keep.close()


CONSTS = 5 + 1 + 2 * NL + 2
SETUP = 1


def turn_slot(ps, k):
    return ps[:, 2 * (k % 4):2 * (k % 4) + 2, :].rearrange("p a b -> p (a b)")


def tok_slot(ps, c):
    return ps[:, 2 * (c % 4):2 * (c % 4) + 2, :].rearrange("p a b -> p (a b)")


_INS = ["x_prompt", "x_sample", "state_gla", "state_hgrn", "norm_mix_pre", "norm_mix_post", "norm_ffn_pre",
        "norm_ffn_post", "w_in", "gla_w_lr2", "gla_b_lr", "gla_onorm", "hgrn_lb", "hgrn_onorm", "w_out",
        "w_ffn_in", "w_ffn_out"]
_BY_FEATURE = ("norm_mix_pre", "gla_b_lr", "gla_onorm", "hgrn_lb", "hgrn_onorm")
_OUTS = [((1, 512, 1024), "float32"), ((8, 8, 1024), "float32"), ((1, 1, 4, 128, 256), "float32"),
         ((1, 8, 4, 128, 256), "float32"), ((1, 1, 8, 128, 128), "float32"), ((1, 8, 8, 128, 128), "float32")]


def kernel(**inputs):
    import numpy as _np
    import concourse.bacc as _bacc
    from concourse import mybir as _mybir
    from concourse.bass_utils import run_bass_kernel_spmd as _run

    nc = _bacc.Bacc("TRN2", target_bir_lowering=False, num_devices=1)
    arrays, args = {}, []
    for name in _INS:
        a = inputs[name]
        if name in _BY_FEATURE:
            a = _np.asarray(a).reshape(-1, 128).T
        a = _np.ascontiguousarray(a)
        arrays[f"in_{name}_dram"] = a
        args.append(nc.dram_tensor(f"in_{name}_dram", a.shape, _mybir.dt.from_np(a.dtype), kind="ExternalInput").ap())
    for i, (shape, dtype) in enumerate(_OUTS):
        dt = _mybir.dt.from_np(_np.dtype(dtype))
        args.append(nc.dram_tensor(f"out_{i}_dram", shape, dt, kind="ExternalOutput").ap())
    build(nc, *args)
    r = _run(nc, [arrays], core_ids=[0])
    return tuple(r.results[0][f"out_{i}_dram"] for i in range(len(_OUTS)))
```
